# Optimizing a Trainium2 kernel written in Bass

```python
import math
import jax, jax.numpy as jnp
from jax import lax
import numpy as np

D_MODEL = 1024
BATCH = 1
SEQ = 512
DEPTH = 1

SSD_INNER = D_MODEL
SSD_HEADS = 16
SSD_HEAD_DIM = SSD_INNER // SSD_HEADS
SSD_GROUPS = 2
SSD_STATE = 128
SSD_CONV = 4
SSD_CHUNK = 128
SSD_XBC = SSD_INNER + 2 * SSD_GROUPS * SSD_STATE

SB_HEADS = 16
SB_HEAD_DIM = 64
SB_WIDTH = SB_HEADS * SB_HEAD_DIM
SB_BLOCK = 128

MIX_WIDTH = SSD_INNER + SB_WIDTH
IN_PROJ = SSD_INNER + SSD_XBC + SSD_HEADS + 3 * SB_WIDTH

MEM_TOKENS = 256
MEM_HEADS = 4
MEM_HEAD_DIM = D_MODEL // MEM_HEADS

D_FF = 2816
FFN_CONV = 3

EPS = 1e-6

kernel_name = "hymba_ssd_stickbreaking_hybrid_layer"

def rmsnorm(x, w):
    xf = x.astype(jnp.float32)
    y = xf * lax.rsqrt(jnp.mean(xf * xf, axis=-1, keepdims=True) + EPS)
    return y.astype(x.dtype) * w

def causal_dwconv(x, w, b):
    K, C = w.shape
    y = lax.conv_general_dilated(
        x, w[:, None, :].astype(x.dtype), window_strides=(1,), padding=[(K - 1, 0)],
        dimension_numbers=("NWC", "WIO", "NWC"), feature_group_count=C)
    return y + b

def ssd_chunked(xh, dt, A, Bh, Ch):
    b, l, h, p = xh.shape
    n = Bh.shape[-1]
    c = l // SSD_CHUNK
    L = SSD_CHUNK
    dtype = xh.dtype
    a = dt * A
    xc = (xh * dt[..., None].astype(dtype)).reshape(b, c, L, h, p)
    Bc = Bh.reshape(b, c, L, h, n)
    Cc = Ch.reshape(b, c, L, h, n)
    a_cs = jnp.cumsum(a.reshape(b, c, L, h).transpose(0, 3, 1, 2), axis=-1)
    seg = a_cs[..., :, None] - a_cs[..., None, :]
    tril = jnp.tril(jnp.ones((L, L), dtype=bool))
    Lmat = jnp.where(tril, jnp.exp(jnp.where(tril, seg, 0.0)), 0.0).astype(dtype)
    cb = jnp.einsum("bclhn,bcshn->bhcls", Cc, Bc) * Lmat
    y_diag = jnp.einsum("bhcls,bcshp->bclhp", cb, xc)
    decay_states = jnp.exp(a_cs[..., -1:] - a_cs).astype(dtype)
    states = jnp.einsum("bclhn,bhcl,bclhp->bchpn", Bc, decay_states, xc)
    chunk_decay = jnp.exp(a_cs[..., -1]).astype(dtype)

    def step(carry, inp):
        s, d = inp
        return carry * d[..., None, None] + s, carry

    init = jnp.zeros((b, h, p, n), dtype=states.dtype)
    _, prev = lax.scan(step, init, (states.transpose(1, 0, 2, 3, 4), chunk_decay.transpose(2, 0, 1)))
    prev = prev.transpose(1, 0, 2, 3, 4)
    y_off = jnp.einsum("bclhn,bchpn,bhcl->bclhp", Cc, prev, jnp.exp(a_cs).astype(dtype))
    return (y_diag + y_off).reshape(b, l, h, p)

def ssd_mixer(z, xbc, dt_raw, conv_w, conv_b, dt_bias, a_log, d_skip, norm_w):
    b, l, _ = xbc.shape
    xbc = jax.nn.silu(causal_dwconv(xbc, conv_w, conv_b))
    xs = xbc[..., :SSD_INNER]
    Bm = xbc[..., SSD_INNER:SSD_INNER + SSD_GROUPS * SSD_STATE].reshape(b, l, SSD_GROUPS, SSD_STATE)
    Cm = xbc[..., SSD_INNER + SSD_GROUPS * SSD_STATE:].reshape(b, l, SSD_GROUPS, SSD_STATE)
    rep = SSD_HEADS // SSD_GROUPS
    Bh = jnp.repeat(Bm, rep, axis=2)
    Ch = jnp.repeat(Cm, rep, axis=2)
    xh = xs.reshape(b, l, SSD_HEADS, SSD_HEAD_DIM)
    dt = jax.nn.softplus((dt_raw + dt_bias).astype(jnp.float32))
    A = -jnp.exp(a_log.astype(jnp.float32))
    y = ssd_chunked(xh, dt, A, Bh, Ch)
    y = y + xh * d_skip[:, None]
    y = y.reshape(b, l, SSD_INNER) * jax.nn.silu(z)
    yg = y.reshape(b, l, SSD_GROUPS, SSD_INNER // SSD_GROUPS)
    yg = rmsnorm(yg, norm_w.reshape(SSD_GROUPS, SSD_INNER // SSD_GROUPS))
    return yg.reshape(b, l, SSD_INNER)

def stick_breaking_attention(q, k, v, norm_w):
    b, S, _ = q.shape
    nb = S // SB_BLOCK
    qh = q.reshape(b, S, SB_HEADS, SB_HEAD_DIM).transpose(0, 2, 1, 3)
    kh = k.reshape(b, S, SB_HEADS, SB_HEAD_DIM).transpose(0, 2, 1, 3)
    vh = v.reshape(b, S, SB_HEADS, SB_HEAD_DIM).transpose(0, 2, 1, 3)
    qb = qh.reshape(b, SB_HEADS, nb, SB_BLOCK, SB_HEAD_DIM).transpose(2, 0, 1, 3, 4)
    starts = jnp.arange(nb, dtype=jnp.int32) * SB_BLOCK
    scale = 1.0 / math.sqrt(SB_HEAD_DIM)
    s_idx = jnp.arange(S, dtype=jnp.int32)

    def block(args):
        qblk, start = args
        zz = jnp.einsum("bhqd,bhkd->bhqk", qblk, kh).astype(jnp.float32) * scale
        t_idx = start + jnp.arange(SB_BLOCK, dtype=jnp.int32)
        causal = s_idx[None, :] < t_idx[:, None]
        lnb = jnp.where(causal, jax.nn.log_sigmoid(-zz), 0.0)
        excl = lax.cumsum(lnb, axis=3, reverse=True) - lnb
        A = jnp.where(causal, jnp.exp(jax.nn.log_sigmoid(zz) + excl), 0.0)
        return jnp.einsum("bhqk,bhkd->bhqd", A.astype(vh.dtype), vh)

    out = lax.map(block, (qb, starts))
    out = out.transpose(1, 0, 3, 2, 4).reshape(b, S, SB_HEADS, SB_HEAD_DIM)
    out = rmsnorm(out, norm_w.reshape(SB_HEADS, SB_HEAD_DIM))
    return out.reshape(b, S, SB_WIDTH)

def memory_cross_attention(h, m, w_q, w_k, w_v, w_o):
    b, S, _ = h.shape
    M = m.shape[1]
    q = (h @ w_q).reshape(b, S, MEM_HEADS, MEM_HEAD_DIM)
    k = (m @ w_k).reshape(b, M, MEM_HEADS, MEM_HEAD_DIM)
    v = (m @ w_v).reshape(b, M, MEM_HEADS, MEM_HEAD_DIM)
    sc = jnp.einsum("bshd,bmhd->bhsm", q, k).astype(jnp.float32) / math.sqrt(MEM_HEAD_DIM)
    p = jax.nn.softmax(sc, axis=-1).astype(v.dtype)
    o = jnp.einsum("bhsm,bmhd->bshd", p, v).reshape(b, S, D_MODEL)
    return o @ w_o

def conv_glu_ffn(h, w_up, conv_w, conv_b, w_down):
    u = causal_dwconv(h @ w_up, conv_w, conv_b)
    g, val = u[..., :D_FF], u[..., D_FF:]
    return (jax.nn.silu(g) * val) @ w_down

def setup_inputs(seed: int = 0) -> dict:
    key = jax.random.key(seed)
    ks = jax.random.split(key, 32)
    f32 = jnp.float32

    def nrm(k, shape, fan_in):
        return jax.random.normal(k, shape, f32) * (fan_in ** -0.5)

    def gain(k, shape):
        return 1.0 + 0.02 * jax.random.normal(k, shape, f32)

    Ld = DEPTH
    dt0 = jnp.exp(jax.random.uniform(ks[8], (Ld, SSD_HEADS), f32, math.log(1e-3), math.log(1e-1)))
    dt_bias = dt0 + jnp.log(-jnp.expm1(-dt0))
    return {
        "x": jax.random.normal(ks[0], (BATCH, SEQ, D_MODEL), f32),
        "mem": jax.random.normal(ks[1], (BATCH, MEM_TOKENS, D_MODEL), f32),
        "norm_mix_w": gain(ks[2], (Ld, D_MODEL)),
        "w_in": nrm(ks[3], (Ld, D_MODEL, IN_PROJ), D_MODEL),
        "conv_ssd_w": nrm(ks[4], (Ld, SSD_CONV, SSD_XBC), SSD_CONV),
        "conv_ssd_b": 0.02 * jax.random.normal(ks[5], (Ld, SSD_XBC), f32),
        "dt_bias": dt_bias,
        "a_log": jnp.log(jax.random.uniform(ks[6], (Ld, SSD_HEADS), f32, 1.0, 16.0)),
        "d_skip": gain(ks[7], (Ld, SSD_HEADS)),
        "ssd_norm_w": gain(ks[9], (Ld, SSD_INNER)),
        "sb_norm_w": gain(ks[10], (Ld, SB_WIDTH)),
        "w_out": nrm(ks[11], (Ld, MIX_WIDTH, D_MODEL), MIX_WIDTH),
        "norm_mem_w": gain(ks[12], (Ld, D_MODEL)),
        "norm_memkv_w": gain(ks[13], (Ld, D_MODEL)),
        "w_mq": nrm(ks[14], (Ld, D_MODEL, D_MODEL), D_MODEL),
        "w_mk": nrm(ks[15], (Ld, D_MODEL, D_MODEL), D_MODEL),
        "w_mv": nrm(ks[16], (Ld, D_MODEL, D_MODEL), D_MODEL),
        "w_mo": nrm(ks[17], (Ld, D_MODEL, D_MODEL), D_MODEL),
        "norm_ffn_w": gain(ks[18], (Ld, D_MODEL)),
        "w_up": nrm(ks[19], (Ld, D_MODEL, 2 * D_FF), D_MODEL),
        "conv_ffn_w": nrm(ks[20], (Ld, FFN_CONV, 2 * D_FF), FFN_CONV),
        "conv_ffn_b": 0.02 * jax.random.normal(ks[21], (Ld, 2 * D_FF), f32),
        "w_down": nrm(ks[22], (Ld, D_FF, D_MODEL), D_FF),
        "norm_final_w": gain(ks[23], (D_MODEL,)),
    }

def reference(x, mem, norm_mix_w, w_in, conv_ssd_w, conv_ssd_b, dt_bias, a_log, d_skip,
              ssd_norm_w, sb_norm_w, w_out, norm_mem_w, norm_memkv_w, w_mq, w_mk, w_mv, w_mo,
              norm_ffn_w, w_up, conv_ffn_w, conv_ffn_b, w_down, norm_final_w):
    o1 = SSD_INNER
    o2 = o1 + SSD_XBC
    o3 = o2 + SSD_HEADS
    o4 = o3 + SB_WIDTH
    o5 = o4 + SB_WIDTH
    for l in range(DEPTH):
        h = rmsnorm(x, norm_mix_w[l])
        proj = h @ w_in[l]
        z, xbc, dt_raw = proj[..., :o1], proj[..., o1:o2], proj[..., o2:o3]
        q, k, v = proj[..., o3:o4], proj[..., o4:o5], proj[..., o5:]
        y_ssd = ssd_mixer(z, xbc, dt_raw, conv_ssd_w[l], conv_ssd_b[l], dt_bias[l],
                          a_log[l], d_skip[l], ssd_norm_w[l])
        y_sb = stick_breaking_attention(q, k, v, sb_norm_w[l])
        x = x + jnp.concatenate([y_ssd, y_sb], axis=-1) @ w_out[l]
        h = rmsnorm(x, norm_mem_w[l])
        m = rmsnorm(mem, norm_memkv_w[l])
        x = x + memory_cross_attention(h, m, w_mq[l], w_mk[l], w_mv[l], w_mo[l])
        h = rmsnorm(x, norm_ffn_w[l])
        x = x + conv_glu_ffn(h, w_up[l], conv_ffn_w[l], conv_ffn_b[l], w_down[l])
    return rmsnorm(x, norm_final_w)


_drawn_inputs = setup_inputs


def setup_inputs(seed=0):
    import zlib

    import numpy as np

    out = dict(_drawn_inputs(seed))
    spreads = {}
    factors = {'norm_mix_w': 2.689,
     'conv_ssd_b': 3.778,
     'd_skip': 8.0,
     'ssd_norm_w': 5.396,
     'sb_norm_w': 5.41,
     'norm_mem_w': 8.0,
     'norm_memkv_w': 8.0,
     'norm_ffn_w': 5.13,
     'conv_ffn_b': 4.959,
     'norm_final_w': 2.906}
    for name, (base, spread) in spreads.items():
        noise = np.random.default_rng([zlib.crc32(name.encode()), seed]).standard_normal(out[name].shape)
        drawn = base * np.exp(spread * noise) if base else spread * noise
        out[name] = __import__('jax').numpy.asarray(drawn.astype(out[name].dtype))
    for name, factor in factors.items():
        out[name] = (out[name] * factor).astype(out[name].dtype)
    return out
```

```python
from contextlib import ExitStack

import concourse.bass as bass
from concourse import mybir

ALU = mybir.AluOpType
ACT = mybir.ActivationFunctionType
AX = mybir.AxisListType
F32 = mybir.dt.float32
F32R = mybir.dt.float32r
BF16 = mybir.dt.bfloat16

P = 128
D = 1024
SEQ = 512
NT = SEQ // P
KD = D // P
HEADS = 16
PAIRS = HEADS // 2
HD = 64
GROUPS = 2
GH = HEADS // GROUPS
GW = D // GROUPS
NX = (D + 2 * GROUPS * P) // P
CONV = 4
MEM = 256
MB = MEM // P
MH = 4
MHD = D // MH
DFF = 2816
KF = DFF // P
FCONV = 3
EPS = 1e-6
NEG = -1e30

COL_Z = 0
COL_XBC = D
COL_DT = COL_XBC + NX * P
COL_Q = COL_DT + HEADS
COL_K = COL_Q + D
COL_V = COL_K + D

U_XBC = 0
U_DT = U_XBC + NX // 2
U_Z = U_DT + 1
U_V = U_Z + 4
U_QK = U_V + 4
U_MV = U_QK + PAIRS
U_MK = U_MV + 4
U_OUT = U_MK + 4
U_MQ = U_OUT + 8
U_MO = U_MQ + 4
U_UP = U_MO + 4
U_DOWN = U_UP + KF
DOWN_K = [4] * (KF // 4) + [KF % 4]
U_ALL = U_DOWN + 2 * len(DOWN_K)

C_MIX, C_MEMKV, C_MEM, C_FFN, C_SBN = 0, 8, 16, 24, 32
C_CB, C_CW = 40, 52
C_FW, C_FB = 100, 232
C_ALL = C_FB + 2 * KF

START = [0, 128, 256, 256]
OFF = [0, 512, 896, 1152]
WID = [SEQ - s for s in START]
PACK = OFF[3] + WID[3]
CHUNK = [(0, 512), (512, 384), (896, 512)]
BLOCKS = [[0], [1], [2, 3]]
ORDER = [2, 1, 0]


class Steps:

    def __init__(self, engine, semaphore):
        self.engine, self.semaphore, self.n, self.base = engine, semaphore, 0, 0

    def did(self, instruction):
        self.n += 1
        return instruction.then_inc(self.semaphore, 1)

    def settle(self):
        self.engine.wait_ge(self.semaphore, self.base + self.n)

    def do(self, instruction):
        self.did(instruction)
        self.settle()

    def enter(self, i, per):
        self.before, self.per = self.n, per
        self.base = i * per

    def leave(self, times):
        assert self.n - self.before == self.per, (self.n - self.before, self.per)
        self.base = 0
        self.n = self.before + self.per * times


def hymba_layer(nc, x, mem, norm_mix_w, w_in, conv_ssd_w, conv_ssd_b, dt_bias, a_log, d_skip,
                ssd_norm_w, sb_norm_w, w_out, norm_mem_w, norm_memkv_w, w_mq, w_mk, w_mv, w_mo,
                norm_ffn_w, w_up, conv_ffn_w, conv_ffn_b, w_down, norm_final_w, acs_dram, out):
    with ExitStack() as ctx:
        def sb(name, shape, dt=F32, stack=ctx):
            return stack.enter_context(nc.sbuf_tensor(name, shape, dt))

        def sem(name):
            return ctx.enter_context(nc.semaphore(name))

        raw = sb("w_raw", [P, 2, 2048])
        w_hi = sb("w_hi", [P, 2, 2048], F32R)
        w_lo = sb("w_lo", [P, 2, 2048], F32R)
        a_hi = sb("a_hi", [P, KD, SEQ], F32R)
        a_lo = sb("a_lo", [P, KD, SEQ], F32R)
        ident = sb("ident", [P, P])
        ident_b = sb("ident_b", [P, P], BF16)
        neg_b = sb("neg_b", [P, 2 * P], BF16)
        ones = sb("ones", [P, P])
        head_ones = sb("head_ones", [P, P])
        tri_u = sb("tri_u", [P, P])
        neg_tri = sb("neg_tri", [P, P], F32R)
        neg_one = sb("neg_one", [P, P], F32R)
        par = sb("par", [P, C_ALL])
        eps_t = sb("eps_t", [P, 1])
        ssq = sb("ssq", [P, 8])
        rms = sb("rms", [P, 8])
        rinv = sb("rinv", [P, 8])

        one = ExitStack()
        vx = sb("vx", [P, NX, SEQ], stack=one)
        xn = sb("xn", [P, NT, D], stack=one)
        zy = sb("zy", [P, NT, D], stack=one)
        small = one.enter_context(ExitStack())
        conv_acc = sb("conv_acc", [P, 2, SEQ], stack=small)
        b_nat = sb("b_nat", [P, NT, GROUPS, P], stack=small)
        cb_m = sb("cb_m", [P, GROUPS, P], stack=small)
        seg = sb("seg", [P, 2, HEADS, P], stack=small)
        xdt = sb("xdt", [P, 2, D + HD], stack=small)
        xdd = sb("xdd", [P, D], stack=small)
        xsk = sb("xsk", [P, D], stack=small)
        yt = sb("yt", [P, D], stack=small)
        carry = sb("carry", [P, D], stack=small)
        ssdn_w = sb("ssdn_w", [P, D], stack=small)
        head_b = sb("head_b", [P, 3, HEADS], stack=small)
        sc = sb("sc", [P, 12, NT * HEADS], stack=small)
        mem_nat = sb("mem_nat", [P, MB, D], stack=small)
        small.close()
        dtT, acsT = yt[0:HEADS, 0:SEQ], xsk[0:HEADS, 0:SEQ]
        q_hi = sb("q_hi", [P, 2, SEQ], F32R, one)
        q_lo = sb("q_lo", [P, 2, SEQ], F32R, one)
        k_hi = sb("k_hi", [P, SEQ], F32R, one)
        k_lo = sb("k_lo", [P, SEQ], F32R, one)
        v_hi = sb("v_hi", [P, NT, 3, HD], F32R, one)
        v_lo = sb("v_lo", [P, NT, 3, HD], F32R, one)
        s_hi = sb("s_hi", [P, PACK], F32R, one)
        s_lo = sb("s_lo", [P, PACK], F32R, one)
        p_hi = sb("p_hi", [P, PACK], F32R, one)
        p_lo = sb("p_lo", [P, PACK], F32R, one)
        soft = sb("soft", [P, PACK], F32, one)
        prob = sb("prob", [P, PACK], F32, one)
        one.close()
        v_nat = vx[:, 0:KD, :].rearrange("p c s -> p (c s)").rearrange("p (t d) -> p t d", t=NT)
        ysb = xn[:, :, :].rearrange("p t d -> p (t d)").rearrange("p (c s) -> p c s", c=KD)

        two = ExitStack()
        early = two.enter_context(ExitStack())
        m_hi = sb("m_hi", [P, KD, MEM], F32R, early)
        m_lo = sb("m_lo", [P, KD, MEM], F32R, early)
        x_blk = sb("x_blk", [P, 2, D], F32, early)
        early.close()
        late = two.enter_context(ExitStack())
        sm_p = sb("sm_p", [P, MH, NT, MEM], F32, late)
        pt_hi = sb("pt_hi", [P, MB, SEQ], F32R, late)
        pt_lo = sb("pt_lo", [P, MB, SEQ], F32R, late)
        smx = sb("smx", [P, MH, 3, NT], F32, late)
        late.close()
        h2_hi = sb("h2_hi", [P, KD, SEQ], F32R, two)
        h2_lo = sb("h2_lo", [P, KD, SEQ], F32R, two)
        km_hi = sb("km_hi", [P, KD, MEM], F32R, two)
        vm_hi = sb("vm_hi", [P, MB, D], F32R, two)
        vm_lo = sb("vm_lo", [P, MB, D], F32R, two)
        b_hi = sb("b_hi", [P, KD, SEQ], F32R, two)
        b_lo = sb("b_lo", [P, KD, SEQ], F32R, two)
        xT = sb("xT", [P, KD, SEQ], F32, two)
        two_top = two.enter_context(ExitStack())
        km_lo = sb("km_lo", [P, KD, MEM], F32R, two_top)
        sq = sb("sq", [P, 2, SEQ], F32, two_top)
        acc_s = sb("acc_s", [P, SEQ], F32, two_top)
        sb("gap", [P, 4 * (FCONV - 1 + SEQ) + 4 * SEQ - 2 * KD * MEM // 2 - 3 * SEQ], F32, two_top)
        r_row = sb("r_row", [P, SEQ], F32, two_top)
        two.close()

        three = ExitStack()
        ff_hi = sb("ff_hi", [P, KF, SEQ], F32R, three)
        ff_lo = sb("ff_lo", [P, KF, SEQ], F32R, three)
        three.enter_context(nc.sbuf_tensor("xT_stays", [P, KD, SEQ], F32))
        up = three.enter_context(ExitStack())
        u_pad = sb("u_pad", [P, 2, 2, FCONV - 1 + SEQ], F32, up)
        u_acc = sb("u_acc", [P, 2, 2, SEQ], F32, up)
        up.close()
        fin_w = sb("fin_w", [P, D], F32, three)
        y_out = sb("y_out", [P, 6, SEQ], F32, three)
        three.close()

        ps = ctx.enter_context(nc.psum_tensor("ps", [P, 8, SEQ], F32))

        S = {}
        for name in (
            "x_in0 x_in1 x_in2 x_in3 rows_in bcast_in mem_in raw_in0 raw_in1 fin_in "
            "acs_out seg_in0 seg_in1 xblk_in0 xblk_in1 y_sent0 y_sent1 y_sent "
            "consts consts_r w_hi_ok w_lo_ok w_used tile0_mm "
            "rms_ok x_scaled mem_scaled par_tr par_ok x_tr h_hi_ok h_lo_ok "
            "conv_tap conv_ok conv_silu dtT_ok dt_tr dt_exp dt_ln dt_ok acs_mm "
            "acs_ok acsT_ok decay_ok nat_mm nat_ok xtr_mm xn_even xn_odd cb_mm cb_ok seg_ok seg_exp "
            "m_ok xd_ok diag_mm state_mm y_ok carry_ok y_gated ssd_rms ssd_ok "
            "q_hi_ok q_ok k_hi_ok k_ok v_hi_ok v_ok pad_ok z_mm ln_ok soft_ok cs_mm "
            "prob_ok p_ok av_mm o_ok ytr_mm yh_ok yl_ok mtr_mm mh_ok ml_ok "
            "mk_hi_ok mk_ok mv_mm mv_hi_ok mv_ok sb_sq sb_mm sb_rms sb_y sb_hi_ok sb_ok "
            "res_tr res_ok res_sum res_sq res_hi res_lo row_mm row_rms row_ok "
            "mq_f mq_hi_ok mq_ok sm_mm sm_max sm_exp sm_div pt_mm pt_hi_ok pt_ok o_mm "
            "mo_hi_ok mo_ok up_pad up_tap up_conv up_silu up_f up_hi_ok up_ok "
            "down_mm fin_sq fin_ms fin_rms fin_y act_step dve_step pool_step"
        ).split():
            S[name] = sem(name)
        s = S
        raw_in = [s["raw_in0"], s["raw_in1"]]
        seg_in = [s["seg_in0"], s["seg_in1"]]
        xblk_in = [s["xblk_in0"], s["xblk_in1"]]
        x_in = [s[f"x_in{t}"] for t in range(NT)]
        def y_sent(n):
            return s[f"y_sent{n}"] if n < 2 else s["y_sent"]

        DVE_SC = ["v", "u", "w", "ln", "d", "z", "dt", "a", "acs", "e", "dec", "cd"]

        def col(name):
            return sc[:, DVE_SC.index(name), :]

        def heads_of(name, c, g, width):
            a = col(name)[:, c * HEADS + g * GH:c * HEADS + (g + 1) * GH]
            return a.unsqueeze(2).to_broadcast([P, GH, width])

        def all_heads(name, c, width):
            return col(name)[:, c * HEADS:(c + 1) * HEADS].unsqueeze(2).to_broadcast([P, HEADS, width])

        def k_of(half):
            return slice(4 * half, 4 * half + 4)

        win = w_in[0].rearrange("(k p) n -> p k n", p=P)
        block = ctx.enter_context(nc.Block())

        def tile_done(engine, u, m):
            if m == 0:
                engine.wait_ge(s["tile0_mm"], u + 1)
            else:
                engine.wait_ge(s["w_used"], u + 3)

        def nat_done(engine, h, t):
            if t < NT - 1:
                engine.wait_ge(s["nat_mm"], (NT - 1) * h + t + 1)
            else:
                engine.wait_ge(s["w_used"], U_Z + 2 * h + 1 + 3)

        def mv_done(engine, h, b):
            if b == 0:
                engine.wait_ge(s["mv_mm"], h + 1)
            else:
                engine.wait_ge(s["w_used"], U_MV + 2 * h + 1 + 3)

        def down_done(engine, half, t):
            if t < NT - 1:
                engine.wait_ge(s["down_mm"], (NT - 1) * half + t + 1)
            else:
                engine.wait_ge(s["w_used"], U_DOWN + (half + 1) * len(DOWN_K) - 1 + 3)

        def z_bank(e, j):
            return 2 + 3 * e + j

        def sm_bank(h, t):
            return (2 + 2 * h + t // 2) % 8

        def v_pair(p):
            v4 = v_nat.rearrange("p t (h d) -> p t h d", d=HD)
            return v4[:, :, bass.ds(2 * p, 2), :]

        def conv_w_col(tap, tile):
            return par[:, bass.ds(C_CW + tap * NX + tile, 1)]

        def ffn_w_col(tap, m, tile):
            return par[:, bass.ds(C_FW + tap * 2 * KF + m * KF + tile, 1)]

        SB_ORDER = [4, 5, 6, 7, 0, 1, 2, 3]

        @block.sync
        def _(sp):
            sp.sem_inc(s["w_lo_ok"], 2)

            def unit(u, parity, parts):
                sp.wait_ge(s["w_lo_ok"], u + 1)
                for dst, src in parts:
                    sp.dma_start(dst, src).then_inc(raw_in[parity], 16)

            def t_parts(parity, w, c0, rows=0, width=256):
                dst = raw[:, parity].rearrange("p (k n) -> p k n", k=KD)[:, :, 0:width]
                return [(dst[:, k_of(h)], w[:, rows + 4 * h:rows + 4 * h + 4, bass.ds(c0, width)])
                        for h in range(2)]

            def n_parts(parity, w, k0, kn, c0):
                dst = raw[:, parity].rearrange("p (k n) -> p k n", k=4)
                half = kn // 2
                return [(dst[:, h * half:(h + 1) * half], w[:, k0 + h * half:k0 + (h + 1) * half, c0:c0 + 512])
                        for h in range(2)]

            def two_tiles(parity, w, c0, c1):
                dst = raw[:, parity].rearrange("p (k m n) -> p k m n", k=KD, m=2)
                return [(dst[:, :, m], w[:, :, bass.ds(c, P)]) for m, c in enumerate((c0, c1))]

            for t in range(NT):
                sp.dma_start(xn[:, t, :], x[0, t * P:(t + 1) * P, :]).then_inc(x_in[t], 16)
            with sp.Fori(0, NX // 4) as i:
                for j in range(2):
                    unit(2 * i + j, j, t_parts(j, win, COL_XBC + 512 * i + 256 * j))
            unit(U_DT, U_DT % 2, t_parts(U_DT % 2, win, COL_DT, width=HEADS))

            def seg_load(c):
                if c >= 2:
                    sp.wait_ge(s["diag_mm"], 2 * (c - 1))
                sp.dma_start(seg[:, c % 2], acs_dram[c:c + 1].to_broadcast([P, HEADS, P])
                             ).then_inc(seg_in[c % 2], 16)

            for n in range(8):
                u = U_Z + n
                base, half, kh = (COL_Z if n < 4 else COL_V), (n % 4) // 2, n % 2
                unit(u, u % 2, n_parts(u % 2, win, 4 * kh, 4, base + 512 * half))
                if n == 2:
                    sp.wait_ge(s["acsT_ok"], 1)
                    sp.dma_start(acs_dram.rearrange("c h l -> h c l"),
                                 acsT.rearrange("h (c l) -> h c l", c=NT)).then_inc(s["acs_out"], 16)
                if n == 3:
                    sp.wait_ge(s["acs_out"], 16)
                    seg_load(0)
                    seg_load(1)
                if n == 7:
                    seg_load(2)
            unit(U_QK, U_QK % 2, two_tiles(U_QK % 2, win, COL_Q, COL_K))
            seg_load(3)
            unit(U_QK + 1, (U_QK + 1) % 2, two_tiles((U_QK + 1) % 2, win, COL_Q + P, COL_K + P))
            with sp.Fori(0, 3) as i:
                for j in range(2):
                    u0 = U_QK + 2 + j
                    unit(u0 + 2 * i, u0 % 2, two_tiles(u0 % 2, win, COL_Q + (2 + j) * P + 2 * P * i,
                                                       COL_K + (2 + j) * P + 2 * P * i))
            wmk = w_mk[0].rearrange("(k p) n -> p k n", p=P)
            wmv = w_mv[0].rearrange("(k p) n -> p k n", p=P)

            def input_block(n):
                if n == 0:
                    sp.wait_ge(s["av_mm"], HEADS)
                if n >= 2:
                    sp.wait_ge(s["res_tr"], 2 * (n - 1))
                sp.dma_start(x_blk[:, n % 2], x[0, n * P:(n + 1) * P, :]).then_inc(xblk_in[n % 2], 16)

            for n in range(4):
                u = U_MV + n
                unit(u, u % 2, n_parts(u % 2, wmv, 4 * (n % 2), 4, 512 * (n // 2)))
            input_block(0)
            input_block(1)
            for n in range(4):
                u = U_MK + n
                unit(u, u % 2, t_parts(u % 2, wmk, 256 * n))
                if n >= 2:
                    input_block(n)
            wout = w_out[0].rearrange("(k p) n -> p k n", p=P)
            with sp.Fori(0, 4) as i:
                for j in range(2):
                    u0 = U_OUT + j
                    unit(u0 + 2 * i, u0 % 2, t_parts(u0 % 2, wout, 256 * i, rows=KD * j))
            for first, w in ((U_MQ, w_mq), (U_MO, w_mo)):
                wv = w[0].rearrange("(k p) n -> p k n", p=P)
                with sp.Fori(0, 2) as i:
                    for j in range(2):
                        u0 = first + j
                        unit(u0 + 2 * i, u0 % 2, t_parts(u0 % 2, wv, 512 * i + 256 * j))
            wup = w_up[0].rearrange("(k p) n -> p k n", p=P)
            with sp.Fori(0, KF // 2) as i:
                for j in range(2):
                    u0 = U_UP + j
                    unit(u0 + 2 * i, u0 % 2, two_tiles(u0 % 2, wup, 2 * P * i + P * j, DFF + 2 * P * i + P * j))
            wdn = w_down[0].rearrange("(k p) n -> p k n", p=P)
            for half in range(2):
                for n, kn in enumerate(DOWN_K):
                    u = U_DOWN + half * len(DOWN_K) + n
                    unit(u, u % 2, n_parts(u % 2, wdn, 4 * n, kn, 512 * half))
            sp.wait_ge(s["up_ok"], KF + 2)
            sp.dma_start(fin_w[:], norm_final_w.unsqueeze(0).to_broadcast([P, D])).then_inc(s["fin_in"], 16)
            for n in range(2 * NT):
                half, t = n // NT, n % NT
                sp.wait_ge(s["fin_y"], n + 1)
                sp.dma_start(out[0, t * P:(t + 1) * P, half * 512:(half + 1) * 512], y_out[:, n % 6]
                             ).then_inc(y_sent(n), 16)
            sp.wait_ge(s["y_sent0"], 16)
            sp.wait_ge(s["y_sent1"], 16)
            sp.wait_ge(s["y_sent"], 16 * (2 * NT - 2))

        @block.gpsimd
        def _(pool):
            step = Steps(pool, s["pool_step"])
            tmp = conv_acc

            def select(out_ap, pattern, fill, compare, multiplier, base=0):
                return pool.affine_select(out=out_ap, in_=out_ap, compare_op=compare, fill=fill, base=base,
                                          pattern=pattern, channel_multiplier=multiplier)

            step.did(pool.memset(ident[:], 0.0))
            step.did(pool.memset(tri_u[:], 1.0))
            step.did(pool.memset(tmp[:, 0, 0:P], -1.0))
            step.did(pool.memset(tmp[:, 1, 0:2 * P], 0.0))
            step.did(pool.memset(head_ones[:], 0.0))
            step.settle()
            select(ident[:], [[-1, P]], 1.0, ALU.not_equal, 1).then_inc(s["consts"], 1)
            select(tri_u[:], [[1, P]], 0.0, ALU.is_ge, -1).then_inc(s["consts"], 1)
            select(tmp[:, 0, 0:P], [[-1, P]], 0.0, ALU.is_ge, 1).then_inc(s["consts"], 1)
            step.do(pool.memset(tmp[:, 1, 0:P], NEG))
            select(tmp[:, 1, P:2 * P], [[1, P]], NEG, ALU.is_gt, -1).then_inc(s["consts"], 1)
            pool.memset(tmp[:, 0, P:2 * P], -1.0).then_inc(s["consts"], 1)
            pool.wait_ge(s["consts"], 5)
            pool.memset(head_ones[0:HD, 0:HD], 1.0).then_inc(s["consts"], 1)
            pool.wait_ge(s["consts"], 6)
            pool.memset(head_ones[HD:P, HD:P], 1.0).then_inc(s["consts"], 1)
            pool.wait_ge(s["consts"], 7)
            pool.memset(ones[:], 1.0).then_inc(s["consts"], 1)
            pool.memset(eps_t[:], EPS).then_inc(s["consts"], 1)
            pool.memset(xdt[:, :, D:D + HD], 0.0).then_inc(s["consts"], 1)

            def lo(u, parity, cycle):
                pool.wait_ge(raw_in[parity], 32 * cycle)
                pool.wait_ge(s["w_hi_ok"], u + 1)
                pool.wait_ge(s["w_used"], u + 1)
                pool.tensor_tensor(w_lo[:, parity], raw[:, parity], w_hi[:, parity].bitcast(F32),
                                   ALU.subtract).then_inc(s["w_lo_ok"], 1)

            def lo_at(u):
                lo(u, u % 2, u // 2 + 1)

            def ssd_inputs(c):
                xc = xn[:, c].rearrange("p (h d) -> p h d", h=HEADS)
                xd = xdt[:, c % 2, 0:D].rearrange("p (h d) -> p h d", h=HEADS)
                if c == 0:
                    pool.wait_ge(s["xn_even"], 4)
                    pool.wait_ge(s["xn_odd"], 6)
                    pool.wait_ge(s["acs_out"], 16)
                    pool.wait_ge(s["decay_ok"], 3)
                    pool.wait_ge(s["bcast_in"], 64)
                if c >= 2:
                    pool.wait_ge(s["diag_mm"], 2 * (c - 1))
                pool.tensor_tensor(xd, xc, all_heads("dt", c, HD), ALU.mult).then_inc(s["xd_ok"], 1)
                if c >= 1:
                    pool.wait_ge(s["y_ok"], 2 * c)
                pool.tensor_tensor(xsk[:].rearrange("p (h d) -> p h d", h=HEADS), xc,
                                   head_b[:, 2].unsqueeze(2).to_broadcast([P, HEADS, HD]),
                                   ALU.mult).then_inc(s["xd_ok"], 1)
                if c < NT - 1:
                    pool.wait_ge(s["xd_ok"], 3 * c + 1)
                    if c >= 1:
                        pool.wait_ge(s["state_mm"], 2 * c)
                    pool.tensor_tensor(xdd[:].rearrange("p (h d) -> p h d", h=HEADS), xd,
                                       all_heads("dec", c, HD), ALU.mult).then_inc(s["xd_ok"], 1)

            with pool.Fori(0, 5) as i:
                for j in range(2):
                    lo(2 * i + j, j, i + 1)
            for u in range(10, 14):
                lo_at(u)
                ssd_inputs(u - 10)
            lo_at(14)
            lo_at(15)
            pool.wait_ge(s["ssd_ok"], 8)
            pool.wait_ge(s["w_lo_ok"], 16 + 2)
            for n, t in enumerate((q_hi, q_lo)):
                if n:
                    pool.wait_ge(s["pad_ok"], 2)
                pool.memset(t[HD:P, 0, :].bitcast(F32), 0.0).then_inc(s["pad_ok"], 1)
                pool.wait_ge(s["pad_ok"], 2 * n + 1)
                pool.memset(t[0:HD, 1, :].bitcast(F32), 0.0).then_inc(s["pad_ok"], 1)
            pool.wait_ge(s["pad_ok"], 4)
            for t in (v_hi, v_lo):
                pool.memset(t[:, :, 1, :].bitcast(F32), 0.0).then_inc(s["pad_ok"], 1)

            def pair(p, u0, i):
                pool.wait_ge(s["v_hi_ok"], p + 1)
                pool.tensor_tensor(v_lo[:, :, 0::2, :], v_pair(p), v_hi[:, :, 0::2, :].bitcast(F32),
                                   ALU.subtract).then_inc(s["v_ok"], 1)
                if u0 is not None:
                    lo(u0 + 2 * i, u0 % 2, u0 // 2 + 1 + i)

            lo_at(16)
            pair(0, 17, 0)
            with pool.Fori(0, 3) as i:
                for j in range(2):
                    pair(1 + j + 2 * i, 18 + j, i)
            pair(7, 24, 0)
            assert U_ALL % 2 == 1
            with pool.Fori(0, (U_ALL - 25) // 2) as i:
                for j in range(2):
                    u0 = 25 + j
                    lo(u0 + 2 * i, u0 % 2, u0 // 2 + 1 + i)

        @block.scalar
        def _(act):
            step = Steps(act, s["act_step"])

            def copy_scaled(dst, src, scale=1.0):
                return act.activation(dst, src, ACT.Copy, scale=scale)

            def hi(u, parity, cycle):
                act.wait_ge(raw_in[parity], 32 * cycle)
                act.wait_ge(s["w_used"], u + 1)
                act.copy(w_hi[:, parity], raw[:, parity]).then_inc(s["w_hi_ok"], 1)

            def hi_at(u):
                hi(u, u % 2, u // 2 + 1)

            rows = zy
            n_rows = 0
            for t0, r0, w in ((0, C_MIX, norm_mix_w), (0, C_MEMKV, norm_memkv_w), (0, C_MEM, norm_mem_w),
                              (0, C_FFN, norm_ffn_w), (0, C_SBN, sb_norm_w), (0, C_CB, conv_ssd_b)):
                v = w.rearrange("o (k p) -> (o k) p", p=P)
                act.dma_start(rows[r0:r0 + v.shape[0], t0, 0:P], v).then_inc(s["rows_in"], 16)
                n_rows += 1
            cw = conv_ssd_w[0].rearrange("t (k p) -> (t k) p", p=P)
            act.dma_start(rows[C_CW:C_CW + CONV * NX, 0, 0:P], cw).then_inc(s["rows_in"], 16)
            fw = conv_ffn_w[0].rearrange("t (k p) -> (t k) p", p=P)
            fb = conv_ffn_b.rearrange("o (k p) -> (o k) p", p=P)
            act.dma_start(rows[0:4 * KF, 1, 0:P], fw[0:4 * KF]).then_inc(s["rows_in"], 16)
            act.dma_start(rows[0:2 * KF, 2, 0:P], fw[4 * KF:6 * KF]).then_inc(s["rows_in"], 16)
            act.dma_start(rows[2 * KF:4 * KF, 2, 0:P], fb).then_inc(s["rows_in"], 16)
            act.dma_start(mem_nat[:], mem[0].rearrange("(b p) d -> p b d", p=P)).then_inc(s["mem_in"], 16)
            for n, w in enumerate((dt_bias, a_log, d_skip)):
                act.dma_start(head_b[:, n], w.to_broadcast([P, HEADS])).then_inc(s["bcast_in"], 16)
            act.dma_start(ssdn_w[:], ssd_norm_w.to_broadcast([P, D])).then_inc(s["bcast_in"], 16)

            act.wait_ge(s["consts"], 10)
            act.copy(neg_tri[:], conv_acc[:, 0, 0:P]).then_inc(s["consts_r"], 1)
            act.copy(neg_one[:], conv_acc[:, 0, P:2 * P]).then_inc(s["consts_r"], 1)
            act.copy(neg_b[:], conv_acc[:, 1, 0:2 * P]).then_inc(s["consts_r"], 1)
            act.copy(ident_b[:], ident[:]).then_inc(s["consts_r"], 1)

            for t in range(NT):
                act.wait_ge(x_in[t], 16)
                step.did(act.activation(vx[:, 2 * t:2 * t + 2, :].rearrange("p a b -> p (a b)"), xn[:, t],
                                        ACT.Square, accum_out=ssq[:, t:t + 1]))
            act.wait_ge(s["mem_in"], 16)
            for b in range(MB):
                step.did(act.activation(vx[:, 8 + 2 * b:10 + 2 * b, :].rearrange("p a b -> p (a b)"),
                                        mem_nat[:, b], ACT.Square, accum_out=ssq[:, NT + b:NT + b + 1]))
            step.settle()
            act.activation(rms[:, 0:NT + MB], ssq[:, 0:NT + MB], ACT.Sqrt, scale=1.0 / D, bias=eps_t[:]
                           ).then_inc(s["rms_ok"], 1)
            hi_at(0)
            act.wait_ge(s["par_tr"], 1)
            act.copy(par[:], ps[:, 7, 0:C_ALL]).then_inc(s["par_ok"], 1)
            act.wait_ge(s["par_ok"], 1)
            for c in range(KD):
                act.wait_ge(s["x_tr"], c + 1)
                copy_scaled(a_hi[:, c], ps[:, c], par[:, C_MIX + c:C_MIX + c + 1]).then_inc(s["h_hi_ok"], 1)

            act.sem_inc(s["conv_silu"], 2)
            with act.Fori(0, NX // 4) as i:
                for j in range(4):
                    n = 4 * i + j
                    if j % 2 == 0:
                        u0 = 1 + j // 2
                        hi(u0 + 2 * i, u0 % 2, u0 // 2 + 1 + i)
                    tile_done(act, 2 * i + j // 2, j % 2)
                    act.wait_ge(s["conv_silu"], n + 1)
                    act.activation(conv_acc[:, j % 2], ps[:, j % 2], ACT.Identity, scale=conv_w_col(CONV - 1, n),
                                   bias=par[:, bass.ds(C_CB + n, 1)]).then_inc(s["conv_tap"], 1)
                    act.wait_ge(s["conv_ok"], n + 3)
                    act.activation(vx[:, bass.ds(n, 1), :], conv_acc[:, j % 2:j % 2 + 1, :], ACT.Silu
                                   ).then_inc(s["conv_silu"], 1)
            hi_at(7)
            act.wait_ge(s["dt_ok"], 1)
            step.do(act.activation(col("z"), col("v"), ACT.Abs))
            act.activation(col("u"), col("z"), ACT.Exp, scale=-1.0).then_inc(s["dt_exp"], 1)
            act.wait_ge(s["bcast_in"], 64)
            act.activation(head_b[:, 1], head_b[:, 1], ACT.Exp).then_inc(s["dt_exp"], 1)
            act.wait_ge(s["dt_ok"], 2)
            act.activation(col("ln"), col("w"), ACT.Ln).then_inc(s["dt_ln"], 1)
            hi_at(8)
            act.wait_ge(s["acs_ok"], 3)
            act.activation(col("e"), col("acs"), ACT.Exp).then_inc(s["decay_ok"], 1)
            act.activation(col("dec"), col("dec"), ACT.Exp).then_inc(s["decay_ok"], 1)
            act.activation(col("cd"), col("cd"), ACT.Exp).then_inc(s["decay_ok"], 1)

            def nat_evac(h):
                for t in range(NT):
                    nat_done(act, h, t)
                    if h < 2:
                        act.activation(zy[:, t, 512 * h:512 * h + 512], ps[:, t], ACT.Silu).then_inc(s["nat_ok"], 1)
                    else:
                        act.copy(v_nat[:, t, 512 * (h - 2):512 * (h - 1)], ps[:, t]).then_inc(s["nat_ok"], 1)

            def seg_exp(c):
                act.wait_ge(s["seg_ok"], c + 1)
                act.activation(seg[:, c % 2], seg[:, c % 2], ACT.Exp).then_inc(s["seg_exp"], 1)

            def gated_squares(c):
                for g in range(GROUPS):
                    act.wait_ge(s["y_gated"], 2 * c + g + 1)
                    step.did(act.activation(conv_acc[:, 0], zy[:, c, g * GW:(g + 1) * GW], ACT.Square,
                                            accum_out=ssq[:, 2 * c + g:2 * c + g + 1]))
                    step.settle()

            hi_at(9)
            nat_evac(0)
            hi_at(10)
            for c in range(0, KD, 2):
                act.wait_ge(s["xtr_mm"], c + 1)
                act.copy(xn[:, :, c * P:(c + 1) * P], ps[:, 4 + c % 4].rearrange("p (t n) -> p t n", t=NT)
                         ).then_inc(s["xn_even"], 1)
            seg_exp(0)
            hi_at(11)
            nat_evac(1)
            seg_exp(1)
            hi_at(12)
            gated_squares(0)
            seg_exp(2)
            hi_at(13)
            nat_evac(2)
            gated_squares(1)
            seg_exp(3)
            hi_at(14)
            gated_squares(2)
            hi_at(15)
            nat_evac(3)
            gated_squares(3)
            act.activation(rms[:, 0:8], ssq[:, 0:8], ACT.Sqrt, scale=1.0 / GW, bias=eps_t[:]
                           ).then_inc(s["ssd_rms"], 1)
            hi_at(16)

            def q_evac(p):
                tile_done(act, U_QK + p, 0)
                if isinstance(p, int) and p == 0:
                    act.wait_ge(s["pad_ok"], 6)
                act.wait_ge(s["z_mm"], 6 * p + 6)
                copy_scaled(q_hi[0:HD, 0], ps[0:HD, 0], HD ** -0.5).then_inc(s["q_hi_ok"], 1)
                copy_scaled(q_hi[HD:P, 1], ps[HD:P, 0], HD ** -0.5).then_inc(s["q_hi_ok"], 1)

            def k_evac(p):
                tile_done(act, U_QK + p, 1)
                act.copy(k_hi[:], ps[:, 0]).then_inc(s["k_hi_ok"], 1)

            def softplus(p, e):
                n = 2 * p + e
                for c, j in enumerate(ORDER):
                    o, w = CHUNK[j]
                    act.wait_ge(s["z_mm"], 3 * n + c + 1 + 6)
                    act.wait_ge(s["soft_ok"], 3 * n + c + 1)
                    z = ps[:, z_bank(e, j), 0:w]
                    step.do(act.activation(soft[:, o:o + w], z, ACT.Abs))
                    step.do(act.activation(soft[:, o:o + w], soft[:, o:o + w], ACT.Exp, scale=-1.0))
                    act.activation(soft[:, o:o + w], soft[:, o:o + w], ACT.Ln, bias=1.0).then_inc(s["ln_ok"], 1)

            def probs(p, e):
                n = 2 * p + e
                for c, j in enumerate(ORDER):
                    o, w = CHUNK[j]
                    act.wait_ge(s["cs_mm"], 3 * n + c + 1)
                    act.wait_ge(s["p_ok"], 3 * n + c + 1)
                    act.activation(prob[:, o:o + w], ps[:, z_bank(e, j), 0:w], ACT.Exp).then_inc(s["prob_ok"], 1)

            def o_evac(p):
                act.wait_ge(s["av_mm"], 2 * p + 2)
                act.copy(ysb[:, bass.ds(p, 1), :], ps[:, 1:2, :]).then_inc(s["o_ok"], 1)

            def v_round(p):
                act.wait_ge(s["av_mm"], 2 * p)
                act.copy(v_hi[:, :, 0::2, :], v_pair(p)).then_inc(s["v_hi_ok"], 1)

            def pair(p, u0=None, i=0, first=False):
                last = u0 is None
                softplus(p, 0)
                if not first:
                    o_evac(p - 1)
                    v_round(p)
                if not last:
                    hi(u0 + 2 * i, u0 % 2, u0 // 2 + 1 + i)
                    q_evac(p + 1)
                probs(p, 0)
                if not last:
                    k_evac(p + 1)
                softplus(p, 1)
                probs(p, 1)

            act.sem_inc(s["prob_ok"], 6)
            q_evac(0)
            k_evac(0)
            act.wait_ge(s["nat_ok"], 16)
            act.copy(v_hi[:, :, 0::2, :], v_pair(0)).then_inc(s["v_hi_ok"], 1)
            pair(0, 17, first=True)
            with act.Fori(0, 3) as i:
                step.enter(i, 24)
                for j in range(2):
                    pair(1 + j + 2 * i, 18 + j, i)
                step.leave(3)
            hi_at(24)
            pair(7)

            for c in range(KD):
                act.wait_ge(s["ytr_mm"], c + 1)
                act.copy(a_hi[:, c], ps[:, 2 + c % 2]).then_inc(s["yh_ok"], 1)
            o_evac(7)
            act.wait_ge(s["v_ok"], 8)
            for b in range(4):
                act.wait_ge(s["mtr_mm"], b + 1)
                for c in (2 * b, 2 * b + 1):
                    copy_scaled(m_hi[:, c], ps[:, 4 + b, (c % 2) * MEM:(c % 2 + 1) * MEM],
                                par[:, C_MEMKV + c:C_MEMKV + c + 1]).then_inc(s["mh_ok"], 1)

            def sb_square(n):
                if n >= 1:
                    act.wait_ge(s["sb_mm"], n)
                act.activation(sq[:, 0], ysb[:, SB_ORDER[n]], ACT.Square).then_inc(s["sb_sq"], 1)

            def sb_root(n):
                act.wait_ge(s["sb_mm"], n + 1)
                if n >= 1:
                    act.wait_ge(s["sb_y"], n)
                act.activation(sq[:, 1], ps[:, 6], ACT.Sqrt, scale=1.0 / HD, bias=eps_t[:]).then_inc(s["sb_rms"], 1)

            def sb_round(n):
                act.wait_ge(s["sb_y"], n + 1)
                act.copy(b_hi[:, SB_ORDER[n]], ysb[:, SB_ORDER[n]]).then_inc(s["sb_hi_ok"], 1)

            act.wait_ge(s["o_ok"], 8)
            for n in range(4):
                sb_square(n)
                if n % 2 == 1:
                    h = n // 2
                    for b in range(MB):
                        mv_done(act, h, b)
                        act.copy(vm_hi[:, b, 512 * h:512 * h + 512], ps[:, 2 + 2 * h + b]).then_inc(s["mv_hi_ok"], 1)
                hi_at(U_MV + n + 2)
                sb_root(n)
                sb_round(n)
            for n in range(4):
                sb_square(4 + n)
                for m in range(2):
                    tile_done(act, U_MK + n, m)
                    act.copy(km_hi[:, 2 * n + m], ps[:, m, 0:MEM]).then_inc(s["mk_hi_ok"], 1)
                hi_at(U_MK + n + 2)
                sb_root(4 + n)
                for q in range(2):
                    act.wait_ge(s["res_tr"], 2 * n + q + 1)
                    act.copy(xT[:, 4 * q:4 * q + 4, n * P:(n + 1) * P],
                             ps[:, 7].rearrange("p (c n) -> p c n", c=4)).then_inc(s["res_ok"], 1)
                sb_round(4 + n)

            def residual(n, n8, m, c_gain, dst):
                act.wait_ge(s["res_sum"], n8 + 3)
                act.wait_ge(s["res_lo"], n8 + 1)
                act.activation(sq[:, m:m + 1], xT[:, bass.ds(n, 1)], ACT.Square).then_inc(s["res_sq"], 1)
                copy_scaled(dst[:, bass.ds(n, 1)], xT[:, bass.ds(n, 1)], par[:, bass.ds(c_gain + n, 1)]
                            ).then_inc(s["res_hi"], 1)

            def row_root(n):
                act.wait_ge(s["row_mm"], n + 1)
                act.activation(r_row[:], ps[:, 6], ACT.Sqrt, scale=1.0 / D, bias=eps_t[:]).then_inc(s["row_rms"], 1)

            with act.Fori(0, 4) as i:
                hi(U_OUT + 2 + 2 * i, U_OUT % 2, (U_OUT + 2) // 2 + 1 + i)
                for m in range(2):
                    residual(2 * i + m, 2 * i + m, m, C_MEM, h2_hi)
                hi(U_OUT + 3 + 2 * i, (U_OUT + 1) % 2, (U_OUT + 3) // 2 + 1 + i)
            row_root(0)
            for h in range(MH):
                for m in range(2):
                    c = 2 * h + m
                    act.wait_ge(s["mq_f"], c + 1)
                    act.copy(a_hi[:, c], sq[:, m]).then_inc(s["mq_hi_ok"], 1)
                hi_at(U_MQ + h + 2)
            for h in range(MH):
                for t in range(NT):
                    act.wait_ge(s["sm_max"], 2 * h + t // 2 + 1)
                    act.activation(sm_p[:, h, t], ps[:, sm_bank(h, t), (t % 2) * MEM:(t % 2 + 1) * MEM], ACT.Exp,
                                   bias=smx[:, h, 0, t:t + 1], accum_out=smx[:, h, 1, t:t + 1]
                                   ).then_inc(s["sm_exp"], 1)
            for h in range(MH):
                for b in range(MB):
                    act.wait_ge(s["pt_mm"], 2 * h + b + 1)
                    if h >= 1:
                        act.wait_ge(s["o_mm"], 2 * h)
                    act.copy(pt_hi[:, b], ps[:, 2 + b]).then_inc(s["pt_hi_ok"], 1)
                for m in range(2):
                    act.wait_ge(s["o_mm"], 2 * h + m + 1)
                    act.copy(b_hi[:, 2 * h + m], ps[:, 4 + m]).then_inc(s["mo_hi_ok"], 1)
            with act.Fori(0, 2) as i:
                for j in range(2):
                    for m in range(2):
                        n = 4 * i + 2 * j + m
                        residual(n, KD + n, m, C_FFN, a_hi)
                    u0 = U_MO + j + 2
                    hi(u0 + 2 * i, u0 % 2, u0 // 2 + 1 + i)
            row_root(1)

            act.sem_inc(s["up_tap"], 4)
            with act.Fori(0, KF // 2) as i:
                for j in range(2):
                    n = 2 * i + j
                    for m in range(2):
                        act.wait_ge(s["up_pad"], 2 * n + m + 1 + 4)
                        act.wait_ge(s["up_ok"], n + 1)
                        act.activation(u_acc[:, j, m], u_pad[:, j, m, FCONV - 1:], ACT.Identity,
                                       scale=ffn_w_col(FCONV - 1, m, n),
                                       bias=par[:, bass.ds(C_FB + m * KF + n, 1)]).then_inc(s["up_tap"], 1)
                    u0 = U_UP + j + 2
                    hi(u0 + 2 * i, u0 % 2, u0 // 2 + 1 + i)
                    act.wait_ge(s["up_conv"], 2 * n + 1)
                    act.activation(u_acc[:, j, 0], u_acc[:, j, 0], ACT.Silu).then_inc(s["up_silu"], 1)
                    act.wait_ge(s["up_f"], n + 1)
                    act.copy(ff_hi[:, bass.ds(n, 1)], u_acc[:, j, 0:1]).then_inc(s["up_hi_ok"], 1)
            for half in range(2):
                for n in range(len(DOWN_K)):
                    u = U_DOWN + half * len(DOWN_K) + n + 2
                    if u < U_ALL:
                        hi_at(u)
                for t in range(NT):
                    k = NT * half + t
                    down_done(act, half, t)
                    act.activation(r_row[:], ps[:, k], ACT.Square, accum_out=ssq[:, k:k + 1]
                                   ).then_inc(s["fin_sq"], 1)
                    act.wait_ge(s["fin_sq"], k + 1)
            act.wait_ge(s["fin_ms"], 1)
            act.activation(rms[:, 0:NT], ssq[:, 0:NT], ACT.Sqrt, scale=1.0 / D, bias=eps_t[:]
                           ).then_inc(s["fin_rms"], 1)

        @block.vector
        def _(dve):
            step = Steps(dve, s["dve_step"])

            def minus_hi(dst, src, hi_part):
                return dve.tensor_tensor(dst, src, hi_part.bitcast(F32), ALU.subtract)

            def scaled_minus_hi(dst, src, scale, hi_part):
                return dve.scalar_tensor_tensor(dst, src, scale, hi_part.bitcast(F32), ALU.mult, ALU.subtract)

            dve.sem_inc(s["conv_ok"], 2)
            dve.sem_inc(s["soft_ok"], 3)
            dve.sem_inc(s["p_ok"], 3)
            dve.sem_inc(s["res_sum"], 2)
            dve.sem_inc(s["res_lo"], 2)
            dve.sem_inc(s["up_ok"], 2)
            dve.sem_inc(s["up_pad"], 4)
            dve.wait_ge(s["rms_ok"], 1)
            step.do(dve.reciprocal(rinv[:, 0:NT + MB], rms[:, 0:NT + MB]))
            for t in range(NT):
                dve.tensor_scalar(xn[:, t], xn[:, t], rinv[:, t:t + 1], None, ALU.mult).then_inc(s["x_scaled"], 1)
            for c in range(KD):
                dve.wait_ge(s["h_hi_ok"], c + 1)
                scaled_minus_hi(a_lo[:, c], ps[:, c], par[:, C_MIX + c:C_MIX + c + 1], a_hi[:, c]
                                ).then_inc(s["h_lo_ok"], 1)
            for b in range(MB):
                dve.tensor_scalar(mem_nat[:, b], mem_nat[:, b], rinv[:, NT + b:NT + b + 1], None, ALU.mult
                                  ).then_inc(s["mem_scaled"], 1)

            with dve.Fori(0, NX // 4) as i:
                step.enter(i, 8)
                for j in range(4):
                    n = 4 * i + j
                    dve.wait_ge(s["conv_tap"], n + 1)
                    for tap in range(CONV - 2, -1, -1):
                        d = CONV - 1 - tap
                        acc = conv_acc[:, j % 2, d:]
                        ins = dve.scalar_tensor_tensor(acc, ps[:, j % 2, 0:SEQ - d], conv_w_col(tap, n), acc,
                                                       ALU.mult, ALU.add)
                        if tap:
                            step.do(ins)
                        else:
                            ins.then_inc(s["conv_ok"], 1)
                step.leave(NX // 4)

            tile_done(dve, U_DT, 1)
            dve.tensor_copy(dtT, ps[0:HEADS, 0]).then_inc(s["dtT_ok"], 1)
            dve.wait_ge(s["dt_tr"], 1)
            dve.wait_ge(s["bcast_in"], 64)

            def tok(a):
                return a.rearrange("p (t h) -> p t h", t=NT)

            def per_head(a):
                return a.unsqueeze(1).to_broadcast([P, NT, HEADS])

            dve.tensor_tensor(tok(col("v")), tok(ps[:, 7, 0:NT * HEADS]), per_head(head_b[:, 0]), ALU.add
                              ).then_inc(s["dt_ok"], 1)
            dve.wait_ge(s["dt_exp"], 1)
            dve.tensor_scalar(col("w"), col("u"), 1.0, None, ALU.add).then_inc(s["dt_ok"], 1)
            dve.wait_ge(s["dt_ok"], 2)
            step.do(dve.tensor_scalar(col("d"), col("w"), -1.0, None, ALU.add))
            step.do(dve.tensor_scalar(col("z"), col("d"), 0.0, None, ALU.is_equal))
            step.do(dve.tensor_tensor(col("d"), col("d"), col("z"), ALU.add))
            step.did(dve.reciprocal(col("dec"), col("d")))
            step.did(dve.tensor_tensor(col("z"), col("z"), col("u"), ALU.mult))
            dve.wait_ge(s["dt_ln"], 1)
            step.do(dve.tensor_tensor(col("ln"), col("ln"), col("u"), ALU.mult))
            step.do(dve.tensor_tensor(col("ln"), col("ln"), col("dec"), ALU.mult))
            step.do(dve.tensor_tensor(col("ln"), col("ln"), col("z"), ALU.add))
            step.do(dve.scalar_tensor_tensor(col("dt"), col("v"), 0.0, col("ln"), ALU.max, ALU.add))
            dve.wait_ge(s["dt_exp"], 2)
            dve.scalar_tensor_tensor(tok(col("a")), tok(col("dt")), -1.0, per_head(head_b[:, 1]), ALU.mult, ALU.mult
                                     ).then_inc(s["dt_ok"], 1)
            dve.wait_ge(s["acs_mm"], 1)
            w = NT * HEADS
            dve.tensor_copy(col("acs"), ps[:, 7, w:2 * w]).then_inc(s["acs_ok"], 1)
            dve.wait_ge(s["acs_ok"], 1)
            dve.tensor_tensor(col("dec"), ps[:, 7, 2 * w:3 * w], col("acs"), ALU.subtract).then_inc(s["acs_ok"], 1)
            dve.tensor_copy(col("cd"), ps[:, 7, 2 * w:3 * w]).then_inc(s["acs_ok"], 1)
            dve.wait_ge(s["acs_mm"], 2)
            dve.tensor_copy(acsT, ps[0:HEADS, 6]).then_inc(s["acsT_ok"], 1)
            for c in range(1, KD, 2):
                dve.wait_ge(s["xtr_mm"], c + 1)
                dve.tensor_copy(xn[:, :, c * P:(c + 1) * P], ps[:, 4 + c % 4].rearrange("p (t n) -> p t n", t=NT)
                                ).then_inc(s["xn_odd"], 1)
            for g in range(GROUPS):
                dve.wait_ge(s["xtr_mm"], KD + g + 1)
                dve.tensor_copy(b_nat[:, :, g], ps[:, 4 + g].rearrange("p (t n) -> p t n", t=NT)
                                ).then_inc(s["xn_odd"], 1)

            def seg_sums(c):
                dve.wait_ge(seg_in[c % 2], 16 * (c // 2 + 1))
                step.do(dve.tensor_tensor(seg[:, c % 2], seg[:, c % 2], all_heads("acs", c, P), ALU.subtract))
                dve.tensor_scalar(seg[:, c % 2], seg[:, c % 2], 0.0, None, ALU.min).then_inc(s["seg_ok"], 1)

            def cb_masked(c):
                dve.wait_ge(s["cb_mm"], c + 1)
                if c >= 1:
                    dve.wait_ge(s["m_ok"], 2 * c)
                dve.tensor_tensor(cb_m[:], ps[:, 7, 0:GROUPS * P].rearrange("p (g l) -> p g l", g=GROUPS),
                                  tri_u[:].unsqueeze(1).to_broadcast([P, GROUPS, P]), ALU.mult).then_inc(s["cb_ok"], 1)

            def decayed_cb(c):
                dve.wait_ge(s["seg_exp"], c + 1)
                dve.wait_ge(s["cb_ok"], c + 1)
                for g in range(GROUPS):
                    m = seg[:, c % 2, g * GH:(g + 1) * GH]
                    dve.tensor_tensor(m, m, cb_m[:, g].unsqueeze(1).to_broadcast([P, GH, P]), ALU.mult
                                      ).then_inc(s["m_ok"], 1)

            def ssd_out(c):
                for g in range(GROUPS):
                    gs = slice(g * GW, (g + 1) * GW)
                    yh = yt[:, gs].rearrange("p (h d) -> p h d", h=GH)
                    xh = xsk[:, gs].rearrange("p (h d) -> p h d", h=GH)
                    ch = carry[:, gs].rearrange("p (h d) -> p h d", h=GH)
                    own = ps[:, 4:6].rearrange("p b (h x) -> p (b h) x", x=P)[:, :, 0:HD]
                    dve.wait_ge(s["diag_mm"], 2 * c + g + 1)
                    dve.wait_ge(s["xd_ok"], 3 * c + 2)
                    if c == 0:
                        dve.tensor_tensor(yh, own, xh, ALU.add).then_inc(s["y_ok"], 1)
                    else:
                        step.do(dve.tensor_tensor(yh, ps[:, 6].rearrange("p (h d) -> p h d", h=GH),
                                                  heads_of("e", c, g, HD), ALU.mult))
                        step.do(dve.tensor_tensor(yh, yh, xh, ALU.add))
                        dve.tensor_tensor(yh, own, yh, ALU.add).then_inc(s["y_ok"], 1)
                    if c < NT - 1:
                        dve.wait_ge(s["state_mm"], 2 * c + g + 1)
                        if c == 0:
                            dve.tensor_copy(carry[:, gs], ps[:, 7]).then_inc(s["carry_ok"], 1)
                        else:
                            step.do(dve.tensor_tensor(ch, ch, heads_of("cd", c, g, HD), ALU.mult))
                            dve.tensor_tensor(carry[:, gs], ps[:, 7], carry[:, gs], ALU.add).then_inc(s["carry_ok"], 1)
                    dve.wait_ge(s["y_ok"], 2 * c + g + 1)
                    dve.wait_ge(s["nat_ok"], 2 * NT)
                    dve.tensor_tensor(zy[:, c, gs], zy[:, c, gs], yt[:, gs], ALU.mult).then_inc(s["y_gated"], 1)

            dve.wait_ge(s["acs_ok"], 3)
            seg_sums(0)
            cb_masked(0)
            for c in range(NT):
                decayed_cb(c)
                if c < NT - 1:
                    seg_sums(c + 1)
                if c == 0:
                    dve.wait_ge(s["decay_ok"], 3)
                ssd_out(c)
                if c < NT - 1:
                    cb_masked(c + 1)
            dve.wait_ge(s["ssd_rms"], 1)
            step.do(dve.reciprocal(rinv[:, 0:8], rms[:, 0:8]))
            for c in range(NT):
                for g in range(GROUPS):
                    y = zy[:, c, g * GW:(g + 1) * GW]
                    dve.scalar_tensor_tensor(y, y, rinv[:, 2 * c + g:2 * c + g + 1], ssdn_w[:, g * GW:(g + 1) * GW],
                                             ALU.mult, ALU.mult).then_inc(s["ssd_ok"], 1)

            def q_lo_part(p):
                dve.wait_ge(s["q_hi_ok"], 2 * p + 2)
                scaled_minus_hi(q_lo[0:HD, 0], ps[0:HD, 0], HD ** -0.5, q_hi[0:HD, 0]).then_inc(s["q_ok"], 1)
                scaled_minus_hi(q_lo[HD:P, 1], ps[HD:P, 0], HD ** -0.5, q_hi[HD:P, 1]).then_inc(s["q_ok"], 1)

            def k_lo_part(p):
                dve.wait_ge(s["k_hi_ok"], p + 1)
                minus_hi(k_lo[:], ps[:, 0], k_hi[:]).then_inc(s["k_ok"], 1)

            def softplus(p, e):
                n = 2 * p + e
                for c, j in enumerate(ORDER):
                    o, w = CHUNK[j]
                    dve.wait_ge(s["ln_ok"], 3 * n + c + 1)
                    step.do(dve.scalar_tensor_tensor(soft[:, o:o + w], ps[:, z_bank(e, j), 0:w], 0.0,
                                                     soft[:, o:o + w], ALU.max, ALU.add))
                    if c == 0:
                        dve.wait_ge(s["cs_mm"], 3 * n)
                    step.do(dve.tensor_copy(s_hi[:, o:o + w], soft[:, o:o + w]))
                    minus_hi(s_lo[:, o:o + w], soft[:, o:o + w], s_hi[:, o:o + w]).then_inc(s["soft_ok"], 1)

            def probs(p, e):
                n = 2 * p + e
                for c, j in enumerate(ORDER):
                    o, w = CHUNK[j]
                    dve.wait_ge(s["prob_ok"], 3 * n + c + 1 + 6)
                    if c == 0:
                        dve.wait_ge(s["av_mm"], n)
                    step.do(dve.tensor_copy(p_hi[:, o:o + w], prob[:, o:o + w]))
                    minus_hi(p_lo[:, o:o + w], prob[:, o:o + w], p_hi[:, o:o + w]).then_inc(s["p_ok"], 1)

            def pair(p, last=False):
                softplus(p, 0)
                if not last:
                    q_lo_part(p + 1)
                probs(p, 0)
                if not last:
                    k_lo_part(p + 1)
                softplus(p, 1)
                probs(p, 1)

            dve.wait_ge(s["pad_ok"], 6)
            q_lo_part(0)
            k_lo_part(0)
            pair(0)
            with dve.Fori(0, 3) as i:
                step.enter(i, 2 * 2 * 9)
                for j in range(2):
                    pair(1 + j + 2 * i)
                step.leave(3)
            pair(7, last=True)

            for c in range(KD):
                dve.wait_ge(s["yh_ok"], c + 1)
                minus_hi(a_lo[:, c], ps[:, 2 + c % 2], a_hi[:, c]).then_inc(s["yl_ok"], 1)
            for c in range(KD):
                dve.wait_ge(s["mh_ok"], 2 * (c // 2) + 2)
                scaled_minus_hi(m_lo[:, c], ps[:, 4 + c // 2, (c % 2) * MEM:(c % 2 + 1) * MEM],
                                par[:, C_MEMKV + c:C_MEMKV + c + 1], m_hi[:, c]).then_inc(s["ml_ok"], 1)

            def sb_norm(n):
                c = SB_ORDER[n]
                dve.wait_ge(s["sb_rms"], n + 1)
                step.do(dve.reciprocal(sq[:, 1], sq[:, 1]))
                dve.scalar_tensor_tensor(ysb[:, c], ysb[:, c], par[:, C_SBN + c:C_SBN + c + 1], sq[:, 1],
                                         ALU.mult, ALU.mult).then_inc(s["sb_y"], 1)

            def sb_lo(n):
                c = SB_ORDER[n]
                dve.wait_ge(s["sb_hi_ok"], n + 1)
                minus_hi(b_lo[:, c], ysb[:, c], b_hi[:, c]).then_inc(s["sb_ok"], 1)

            for n in range(4):
                if n % 2 == 1:
                    h = n // 2
                    for b in range(MB):
                        dve.wait_ge(s["mv_hi_ok"], 2 * h + b + 1)
                        minus_hi(vm_lo[:, b, 512 * h:512 * h + 512], ps[:, 2 + 2 * h + b],
                                 vm_hi[:, b, 512 * h:512 * h + 512]).then_inc(s["mv_ok"], 1)
                sb_norm(n)
                sb_lo(n)
            for n in range(4):
                for m in range(2):
                    t = 2 * n + m
                    dve.wait_ge(s["mk_hi_ok"], t + 1)
                    minus_hi(km_lo[:, t], ps[:, m, 0:MEM], km_hi[:, t]).then_inc(s["mk_ok"], 1)
                sb_norm(4 + n)
                sb_lo(4 + n)

            def residual(u, n, n8, m, c_gain, hi_part, lo_part):
                one_tile = bass.ds(n, 1)
                tile_done(dve, u, m)
                dve.tensor_tensor(xT[:, one_tile], ps[:, m:m + 1], xT[:, one_tile], ALU.add).then_inc(s["res_sum"], 1)
                dve.wait_ge(s["res_sq"], n8 + 1)
                step.do(dve.tensor_tensor(acc_s[:], acc_s[:], sq[:, m], ALU.add))
                dve.wait_ge(s["res_hi"], n8 + 1)
                scaled_minus_hi(lo_part[:, one_tile], xT[:, one_tile], par[:, bass.ds(c_gain + n, 1)],
                                hi_part[:, one_tile]).then_inc(s["res_lo"], 1)

            def row_inverse(n):
                dve.wait_ge(s["row_rms"], n + 1)
                dve.reciprocal(r_row[:], r_row[:]).then_inc(s["row_ok"], 1)

            step.do(dve.memset(acc_s[:], 0.0))
            dve.wait_ge(s["res_ok"], 8)
            with dve.Fori(0, 4) as i:
                step.enter(i, 2)
                for m in range(2):
                    residual(U_OUT + 1 + 2 * i, 2 * i + m, 2 * i + m, m, C_MEM, h2_hi, h2_lo)
                step.leave(4)
            row_inverse(0)
            dve.wait_ge(s["row_ok"], 1)
            for h in range(MH):
                for m in range(2):
                    tile_done(dve, U_MQ + h, m)
                    if h:
                        dve.wait_ge(s["mq_ok"], 2 * (h - 1) + m + 1)
                    dve.scalar_tensor_tensor(sq[:, m], ps[:, m], MHD ** -0.5, r_row[:], ALU.mult, ALU.mult
                                             ).then_inc(s["mq_f"], 1)
                for m in range(2):
                    c = 2 * h + m
                    dve.wait_ge(s["mq_hi_ok"], c + 1)
                    minus_hi(a_lo[:, c], sq[:, m], a_hi[:, c]).then_inc(s["mq_ok"], 1)
            for h in range(MH):
                for q in range(2):
                    dve.wait_ge(s["sm_mm"], 2 * h + q + 1)
                    dve.tensor_reduce(smx[:, h, 0, 2 * q:2 * q + 2],
                                      ps[:, sm_bank(h, 2 * q)].rearrange("p (t m) -> p t m", t=2),
                                      AX.X, ALU.max, negate=True).then_inc(s["sm_max"], 1)
            for h in range(MH):
                dve.wait_ge(s["sm_exp"], NT * (h + 1))
                step.do(dve.reciprocal(smx[:, h, 2], smx[:, h, 1]))
                for t in range(NT):
                    dve.tensor_scalar(sm_p[:, h, t], sm_p[:, h, t], smx[:, h, 2, t:t + 1], None, ALU.mult
                                      ).then_inc(s["sm_div"], 1)
            for h in range(MH):
                for b in range(MB):
                    dve.wait_ge(s["pt_hi_ok"], 2 * h + b + 1)
                    minus_hi(pt_lo[:, b], ps[:, 2 + b], pt_hi[:, b]).then_inc(s["pt_ok"], 1)
                for m in range(2):
                    dve.wait_ge(s["mo_hi_ok"], 2 * h + m + 1)
                    minus_hi(b_lo[:, 2 * h + m], ps[:, 4 + m], b_hi[:, 2 * h + m]).then_inc(s["mo_ok"], 1)
            step.do(dve.memset(acc_s[:], 0.0))
            with dve.Fori(0, 2) as i:
                step.enter(i, 4)
                for j in range(2):
                    for m in range(2):
                        n = 4 * i + 2 * j + m
                        residual(U_MO + 2 * i + j, n, KD + n, m, C_FFN, a_hi, a_lo)
                step.leave(2)
            row_inverse(1)

            step.do(dve.memset(u_pad[:, :, :, 0:FCONV - 1], 0.0))
            dve.wait_ge(s["row_ok"], 2)
            with dve.Fori(0, KF // 2) as i:
                step.enter(i, 4)
                for j in range(2):
                    n = 2 * i + j
                    for m in range(2):
                        tile_done(dve, U_UP + n, m)
                        dve.wait_ge(s["up_tap"], 2 * n + m + 1)
                        dve.tensor_tensor(u_pad[:, j, m, FCONV - 1:], ps[:, 2 * j + m], r_row[:], ALU.mult
                                          ).then_inc(s["up_pad"], 1)
                    for m in range(2):
                        dve.wait_ge(s["up_tap"], 2 * n + m + 1 + 4)
                        for tap in range(FCONV - 2, -1, -1):
                            ins = dve.scalar_tensor_tensor(u_acc[:, j, m], u_pad[:, j, m, tap:tap + SEQ],
                                                           ffn_w_col(tap, m, n), u_acc[:, j, m], ALU.mult, ALU.add)
                            if tap:
                                step.do(ins)
                            else:
                                ins.then_inc(s["up_conv"], 1)
                    dve.wait_ge(s["up_silu"], n + 1)
                    dve.wait_ge(s["up_conv"], 2 * n + 2)
                    dve.tensor_tensor(u_acc[:, j, 0], u_acc[:, j, 0], u_acc[:, j, 1], ALU.mult).then_inc(s["up_f"], 1)
                    dve.wait_ge(s["up_hi_ok"], n + 1)
                    minus_hi(ff_lo[:, bass.ds(n, 1)], u_acc[:, j, 0:1], ff_hi[:, bass.ds(n, 1)]).then_inc(s["up_ok"], 1)
                step.leave(KF // 2)

            down_done(dve, 1, NT - 1)
            dve.wait_ge(s["fin_sq"], 2 * NT)
            dve.tensor_tensor(ssq[:, 0:NT], ssq[:, 0:NT], ssq[:, NT:2 * NT], ALU.add).then_inc(s["fin_ms"], 1)
            dve.wait_ge(s["fin_rms"], 1)
            step.do(dve.reciprocal(rinv[:, 0:NT], rms[:, 0:NT]))
            dve.wait_ge(s["fin_in"], 16)
            for n in range(2 * NT):
                half, t = n // NT, n % NT
                if n >= 6:
                    dve.wait_ge(y_sent(n - 6), 16)
                dve.scalar_tensor_tensor(y_out[:, n % 6], ps[:, n], rinv[:, t:t + 1],
                                         fin_w[:, half * 512:(half + 1) * 512], ALU.mult, ALU.mult
                                         ).then_inc(s["fin_y"], 1)

        @block.tensor
        def _(pe):
            def mm(dst, stationary, moving, start, stop, loose=False):
                return pe.matmul(dst, stationary, moving, start=start, stop=stop, skip_group_check=loose)

            def three(dst, st, mv, first, last):
                mm(dst, st[0], mv[0], first, False)
                mm(dst, st[0], mv[1], False, False)
                return mm(dst, st[1], mv[0], False, last)

            def w_tile(parity, k, m, width=P):
                o = k * 2 * P + m * P
                return w_hi[:, parity, o:o + width], w_lo[:, parity, o:o + width]

            def w_row(parity, k):
                return w_hi[:, parity, 512 * k:512 * k + 512], w_lo[:, parity, 512 * k:512 * k + 512]

            def split_in(u):
                pe.wait_ge(s["w_lo_ok"], u + 3)

            def t_unit(u, parity, banks, moving, free=None, first=True, last=True, width=SEQ, ready=None):
                split_in(u)
                for m in range(2):
                    if free is not None:
                        free(m)
                    for k in range(KD):
                        if ready is not None and m == 0:
                            ready(k)
                        ins = three(ps[:, banks[m], 0:width], w_tile(parity, k, m), moving(k),
                                    first and k == 0, last and k == KD - 1)
                    ins.then_inc(s["tile0_mm" if m == 0 else "w_used"], 1)

            def act_tiles(k):
                return a_hi[:, k], a_lo[:, k]

            def b_tiles(k):
                return b_hi[:, k], b_lo[:, k]

            def nat_unit(u, blocks, stationary, bank, k0, kn, first, last, free=None, done=None, loose=False):
                parity = u % 2
                split_in(u)
                for t in range(blocks):
                    if free is not None:
                        free(t)
                    for k in range(kn):
                        st = stationary(k0 + k, t)
                        mv = w_row(parity, k)
                        ins = mm(ps[:, bank + t], st[0], mv[0], first and k == 0, False, loose)
                        if t == 0 and k == 0:
                            ins.then_inc(s["tile0_mm"], 1)
                        mm(ps[:, bank + t], st[0], mv[1], False, False, loose)
                        ins = mm(ps[:, bank + t], st[1], mv[0], False, last and k == kn - 1, loose)
                    if t == blocks - 1:
                        ins.then_inc(s["w_used"], 1)
                    elif done is not None:
                        ins.then_inc(done, 1)

            def flip(dst, src, n=P):
                return pe.transpose(dst, src, ident[0:n, 0:n])

            pe.sem_inc(s["w_used"], 2)
            pe.sem_inc(s["z_mm"], 6)
            pe.wait_ge(s["consts"], 10)
            pe.wait_ge(s["rows_in"], 160)
            flip(ps[:, 7, 0:100], zy[0:100, 0, 0:P], 100)
            flip(ps[:, 7, 100:100 + 4 * KF], zy[0:4 * KF, 1, 0:P], 4 * KF)
            flip(ps[:, 7, 100 + 4 * KF:C_ALL], zy[0:4 * KF, 2, 0:P], 4 * KF).then_inc(s["par_tr"], 1)
            for t in range(NT):
                pe.wait_ge(s["x_scaled"], t + 1)
                for c in range(KD):
                    if t == 0 and c == KD - 1:
                        pe.wait_ge(s["par_ok"], 1)
                    ins = flip(ps[:, c, t * P:(t + 1) * P], xn[:, t, c * P:(c + 1) * P])
                    if t == NT - 1:
                        ins.then_inc(s["x_tr"], 1)

            with pe.Fori(0, NX // 4) as i:
                for j in range(2):
                    t_unit(2 * i + j, j, (0, 1), act_tiles,
                           free=lambda m: pe.wait_ge(s["conv_ok"], 4 * i + 2 * j + m + 1),
                           ready=(lambda k: pe.wait_ge(s["h_lo_ok"], k + 1)) if j == 0 else None)
            split_in(U_DT)
            pe.wait_ge(s["conv_ok"], NX + 1)
            for k in range(KD):
                ins = three(ps[0:HEADS, 0], w_tile(U_DT % 2, k, 0, HEADS), act_tiles(k), k == 0, k == KD - 1)
                if k == 0:
                    ins.then_inc(s["tile0_mm"], 1)
            ins.then_inc(s["w_used"], 1)

            def h_block(k, t):
                return a_hi[:, k, t * P:(t + 1) * P], a_lo[:, k, t * P:(t + 1) * P]

            def zv_unit(n):
                h, q = n // 2, n % 2

                def free(t):
                    if q == 0:
                        if h == 0:
                            pe.wait_ge(s["conv_ok"], NX + 2)
                            pe.wait_ge(s["dtT_ok"], 1)
                        else:
                            pe.wait_ge(s["nat_ok"], NT * (h - 1) + t + 1)
                nat_unit(U_Z + n, NT, h_block, 0, 4 * q, 4, q == 0, q == 1, free=free,
                         done=s["nat_mm"] if q == 1 else None)

            def cb(c):
                if c >= 1:
                    pe.wait_ge(s["carry_ok"], 2 * c)
                for g in range(GROUPS):
                    ins = mm(ps[:, 7, g * P:(g + 1) * P], vx[:, 8 + g, c * P:(c + 1) * P],
                             vx[:, 10 + g, c * P:(c + 1) * P], True, True)
                ins.then_inc(s["cb_mm"], 1)

            def chunk(c):
                for g in range(GROUPS):
                    gs = slice(g * GW, (g + 1) * GW)
                    if c + g:
                        pe.wait_ge(s["y_ok"], 2 * c + g)
                    if c >= 1:
                        pe.wait_ge(s["carry_ok"], 2 * (c - 1) + g + 1)
                        mm(ps[:, 6], vx[:, 10 + g, c * P:(c + 1) * P], carry[:, gs], True, True)
                    pe.wait_ge(s["m_ok"], 2 * c + g + 1)
                    pe.wait_ge(s["xd_ok"], 3 * c + 1)
                    for h in range(GH):
                        o = (g * GH + h) * HD
                        ins = mm(ps[:, 4 + h // 4, (h % 4) * P:(h % 4 + 1) * P], seg[:, c % 2, g * GH + h],
                                 xdt[:, c % 2, o:o + P], True, True)
                    ins.then_inc(s["diag_mm"], 1)
                    if c < NT - 1:
                        pe.wait_ge(s["xd_ok"], 3 * c + 3)
                        if g == 0:
                            pe.wait_ge(s["cb_ok"], c + 1)
                        else:
                            pe.wait_ge(s["carry_ok"], 2 * c + 1)
                        mm(ps[:, 7], b_nat[:, c, g], xdd[:, gs], True, True).then_inc(s["state_mm"], 1)

            pe.wait_ge(s["dtT_ok"], 1)
            for t in range(NT):
                ins = flip(ps[:, 7, t * HEADS:(t + 1) * HEADS], dtT[:, t * P:(t + 1) * P], HEADS)
            ins.then_inc(s["dt_tr"], 1)
            zv_unit(0)
            pe.wait_ge(s["dt_ok"], 3)
            w = NT * HEADS
            mm(ps[:, 7, w:2 * w], tri_u[:], col("a"), True, True)
            mm(ps[:, 7, 2 * w:3 * w], ones[:], col("a"), True, True).then_inc(s["acs_mm"], 1)
            for c in range(NT):
                ins = mm(ps[0:HEADS, 6, c * P:(c + 1) * P], col("a")[:, c * HEADS:(c + 1) * HEADS], tri_u[:], True, True)
            ins.then_inc(s["acs_mm"], 1)
            zv_unit(1)
            pe.wait_ge(s["acs_ok"], 3)
            pe.wait_ge(s["acsT_ok"], 1)
            for c in range(KD):
                pe.wait_ge(s["conv_silu"], c + 3)
                if c >= 4:
                    pe.wait_ge(s["xn_even" if c % 2 == 0 else "xn_odd"], (c - 4) // 2 + 1)
                for t in range(NT):
                    ins = flip(ps[:, 4 + c % 4, t * P:(t + 1) * P], vx[:, c, t * P:(t + 1) * P])
                ins.then_inc(s["xtr_mm"], 1)
            pe.wait_ge(s["conv_silu"], NX + 2)
            for g in range(GROUPS):
                pe.wait_ge(s["xn_odd" if g else "xn_even"], 3)
                for t in range(NT):
                    ins = flip(ps[:, 4 + g, t * P:(t + 1) * P], vx[:, 8 + g, t * P:(t + 1) * P])
                ins.then_inc(s["xtr_mm"], 1)
            zv_unit(2)
            pe.wait_ge(s["xn_even"], 4)
            pe.wait_ge(s["xn_odd"], 6)
            cb(0)
            zv_unit(3)
            for c in range(NT):
                chunk(c)
                if c < NT - 1:
                    cb(c + 1)
                zv_unit(4 + c)

            def scores(p, e):
                n = 2 * p + e
                if e == 0:
                    pe.wait_ge(s["q_ok"], 2 * p + 2)
                    pe.wait_ge(s["k_ok"], p + 1)
                for c, j in enumerate(ORDER):
                    bank = z_bank(e, j)
                    pe.wait_ge(s["prob_ok"], 3 * n + c + 1)
                    for b in BLOCKS[j]:
                        o = (b == 3) * WID[2]
                        dst = ps[:, bank, o:o + WID[b]]
                        key = slice(b * P, (b + 1) * P)
                        mm(dst, k_hi[:, key], q_hi[:, e, START[b]:], b != 3, False, True)
                        mm(dst, k_hi[:, key], q_lo[:, e, START[b]:], False, False, True)
                        mm(dst, k_lo[:, key], q_hi[:, e, START[b]:], False, False, True)
                        if b == 3:
                            ins = mm(ps[:, bank, o:o + 2 * P], ident_b[:], neg_b[:], False, False, True)
                        else:
                            ins = mm(ps[:, bank, o:o + P], ident_b[:], neg_b[:, P:2 * P], False, False, True)
                    ins.then_inc(s["z_mm"], 1)

            def stick_sums(p, e):
                n = 2 * p + e
                for c, j in enumerate(ORDER):
                    bank = z_bank(e, j)
                    pe.wait_ge(s["soft_ok"], 3 * n + c + 1 + 3)
                    for b in BLOCKS[j]:
                        for src in range(b, 4):
                            o = (b == 3) * WID[2] + START[src] - START[b]
                            for part in (s_hi, s_lo):
                                ins = mm(ps[:, bank, o:o + WID[src]], (neg_tri if src == b else neg_one)[:],
                                         part[:, OFF[src]:OFF[src] + WID[src]], False, False, True)
                    ins.then_inc(s["cs_mm"], 1)

            def attend(p, e):
                n = 2 * p + e
                if e == 0:
                    pe.wait_ge(s["o_ok"], p)
                    pe.wait_ge(s["v_ok"], p + 1)
                side = slice(e * HD, e * HD + P)
                vh = v_hi[:].rearrange("p t a d -> p t (a d)")
                vl = v_lo[:].rearrange("p t a d -> p t (a d)")
                for c, j in enumerate(ORDER):
                    pe.wait_ge(s["p_ok"], 3 * n + c + 1 + 3)
                    for b in BLOCKS[j]:
                        dst = ps[:, 1, START[b]:]
                        src = slice(OFF[b], OFF[b] + WID[b])
                        mm(dst, vh[:, b, side], p_hi[:, src], e == 0 and c == 0 and b == 2, False, True)
                        mm(dst, vh[:, b, side], p_lo[:, src], False, False, True)
                        ins = mm(dst, vl[:, b, side], p_hi[:, src], False, False, True)
                ins.then_inc(s["av_mm"], 1)

            def qk_tile(u, parity, m, free=None):
                if m == 0:
                    split_in(u)
                if free is not None:
                    free()
                for k in range(KD):
                    ins = three(ps[:, 0], w_tile(parity, k, m), act_tiles(k), k == 0, k == KD - 1)
                ins.then_inc(s["tile0_mm" if m == 0 else "w_used"], 1)

            def pair(p, u0=None, i=0, first=False):
                scores(p, 0)
                scores(p, 1)
                if not first:
                    attend(p - 1, 1)
                if u0 is not None:
                    qk_tile(u0 + 2 * i, u0 % 2, 0, lambda: pe.wait_ge(s["k_ok"], p + 1))
                stick_sums(p, 0)
                if u0 is not None:
                    qk_tile(u0 + 2 * i, u0 % 2, 1, lambda: pe.wait_ge(s["q_ok"], 2 * p + 4))
                attend(p, 0)
                stick_sums(p, 1)

            pe.wait_ge(s["nat_ok"], 4 * NT)
            qk_tile(U_QK, U_QK % 2, 0)
            qk_tile(U_QK, U_QK % 2, 1, lambda: pe.wait_ge(s["q_ok"], 2))
            pe.wait_ge(s["y_ok"], 2 * NT)
            pe.wait_ge(s["consts_r"], 4)
            pair(0, U_QK + 1, first=True)
            with pe.Fori(0, 3) as i:
                for j in range(2):
                    pair(1 + j + 2 * i, U_QK + 2 + j, i)
            pair(7)

            pe.wait_ge(s["ssd_ok"], 8)
            for c in range(KD):
                if c == 0:
                    pe.wait_ge(s["prob_ok"], 3 * 15 + 6)
                if c >= 2:
                    pe.wait_ge(s["yl_ok"], c - 1)
                for t in range(NT):
                    ins = flip(ps[:, 2 + c % 2, t * P:(t + 1) * P], zy[:, t, c * P:(c + 1) * P])
                ins.then_inc(s["ytr_mm"], 1)
            attend(7, 1)
            pe.wait_ge(s["prob_ok"], 3 * 16 + 6)
            pe.wait_ge(s["mem_scaled"], MB)
            for b in range(4):
                for c in range(2):
                    for t in range(MB):
                        o = c * MEM + t * P
                        ins = flip(ps[:, 4 + b, o:o + P], mem_nat[:, t, (2 * b + c) * P:(2 * b + c + 1) * P])
                ins.then_inc(s["mtr_mm"], 1)

            def head_sums(n):
                pe.wait_ge(s["sb_sq"], n + 1)
                if n >= 1:
                    pe.wait_ge(s["sb_rms"], n)
                mm(ps[:, 6], head_ones[:], sq[:, 0], True, True).then_inc(s["sb_mm"], 1)

            def m_block(k, t):
                return m_hi[:, k, t * P:(t + 1) * P], m_lo[:, k, t * P:(t + 1) * P]

            def m_tiles(k):
                return m_hi[:, k], m_lo[:, k]

            pe.wait_ge(s["yl_ok"], KD)
            pe.wait_ge(s["ml_ok"], KD)
            for n in range(4):
                h, q = n // 2, n % 2
                nat_unit(U_MV + n, MB, m_block, 2 + 2 * h, 4 * q, 4, q == 0, q == 1,
                         done=s["mv_mm"] if q == 1 else None)
                head_sums(n)
            for n in range(4):
                u = U_MK + n
                t_unit(u, u % 2, (0, 1), m_tiles, width=MEM,
                       free=(lambda m: pe.wait_ge(s["mk_ok"], 2 * (n - 1) + m + 1)) if n else None)
                head_sums(4 + n)
                pe.wait_ge(xblk_in[n % 2], 16 * (n // 2 + 1))
                for q in range(2):
                    if n + q:
                        pe.wait_ge(s["res_ok"], 2 * n + q)
                    for c in range(4):
                        ins = flip(ps[:, 7, c * P:(c + 1) * P], x_blk[:, n % 2, (4 * q + c) * P:(4 * q + c + 1) * P])
                    ins.then_inc(s["res_tr"], 1)

            def row_sums(n):
                pe.wait_ge(s["res_lo"], KD * (n + 1) + 2)
                mm(ps[:, 6], ones[:], acc_s[:], True, True).then_inc(s["row_mm"], 1)

            pe.wait_ge(s["mk_ok"], 8)
            pe.wait_ge(s["sb_ok"], 8)
            with pe.Fori(0, 4) as i:
                t_unit(U_OUT + 2 * i, U_OUT % 2, (0, 1), act_tiles, last=False,
                       free=lambda m: pe.wait_ge(s["res_sum"], 2 * i + m + 1))
                t_unit(U_OUT + 1 + 2 * i, (U_OUT + 1) % 2, (0, 1), b_tiles, first=False)
            row_sums(0)

            def h2_tiles(k):
                return h2_hi[:, k], h2_lo[:, k]

            for h in range(MH):
                u = U_MQ + h
                t_unit(u, u % 2, (0, 1), h2_tiles,
                       free=(lambda m: pe.wait_ge(s["mq_f"], 2 * (h - 1) + m + 1)) if h else
                       (lambda m: pe.wait_ge(s["res_sum"], KD + 2)))
            for h in range(MH):
                pe.wait_ge(s["mq_ok"], 2 * h + 2)
                if h == 3:
                    pe.wait_ge(s["mq_f"], 8)
                for t in range(NT):
                    for k in range(2):
                        c = 2 * h + k
                        o = (t % 2) * MEM
                        ins = three(ps[:, sm_bank(h, t), o:o + MEM], h_block(c, t), (km_hi[:, c], km_lo[:, c]),
                                    k == 0, k == 1)
                    if t % 2:
                        ins.then_inc(s["sm_mm"], 1)
            for h in range(MH):
                pe.wait_ge(s["sm_div"], NT * (h + 1))
                if h:
                    pe.wait_ge(s["pt_ok"], 2 * h)
                for b in range(MB):
                    for t in range(NT):
                        ins = flip(ps[:, 2 + b, t * P:(t + 1) * P], sm_p[:, h, t, b * P:(b + 1) * P])
                    ins.then_inc(s["pt_mm"], 1)
                pe.wait_ge(s["sm_exp"], 2 * NT)
                for m in range(2):
                    if h:
                        pe.wait_ge(s["mo_ok"], 2 * (h - 1) + m + 1)
                    for b in range(MB):
                        pe.wait_ge(s["pt_ok"], 2 * h + b + 1)
                        o = h * MHD + m * P
                        ins = three(ps[:, 4 + m], (vm_hi[:, b, o:o + P], vm_lo[:, b, o:o + P]),
                                    (pt_hi[:, b], pt_lo[:, b]), b == 0, b == 1)
                    ins.then_inc(s["o_mm"], 1)
            pe.wait_ge(s["mo_ok"], 8)
            with pe.Fori(0, 2) as i:
                for j in range(2):
                    u0 = U_MO + j
                    t_unit(u0 + 2 * i, u0 % 2, (0, 1), b_tiles,
                           free=lambda m: pe.wait_ge(s["res_sum"], KD + 4 * i + 2 * j + m + 1))
            row_sums(1)
            with pe.Fori(0, KF // 2) as i:
                for j in range(2):
                    u0 = U_UP + j
                    t_unit(u0 + 2 * i, u0 % 2, (2 * j, 2 * j + 1), act_tiles,
                           free=lambda m: pe.wait_ge(s["up_pad"], 4 * i + 2 * j + m + 1))
            pe.wait_ge(s["up_pad"], 2 * KF + 4)
            for half in range(2):
                for t in range(NT):
                    for c in range(4):
                        mm(ps[:, NT * half + t, c * P:(c + 1) * P], xT[:, 4 * half + c, t * P:(t + 1) * P],
                           ident[:], c == 0, False, True)
            pe.wait_ge(s["up_ok"], KF + 2)

            def ff_block(k, t):
                return ff_hi[:, k, t * P:(t + 1) * P], ff_lo[:, k, t * P:(t + 1) * P]

            for half in range(2):
                for n, kn in enumerate(DOWN_K):
                    end = n == len(DOWN_K) - 1
                    nat_unit(U_DOWN + half * len(DOWN_K) + n, NT, ff_block, NT * half, 4 * n, kn, False, end,
                             done=s["down_mm"] if end else None, loose=True)


_NAMES = ["x", "mem", "norm_mix_w", "w_in", "conv_ssd_w", "conv_ssd_b", "dt_bias", "a_log", "d_skip",
          "ssd_norm_w", "sb_norm_w", "w_out", "norm_mem_w", "norm_memkv_w", "w_mq", "w_mk", "w_mv", "w_mo",
          "norm_ffn_w", "w_up", "conv_ffn_w", "conv_ffn_b", "w_down", "norm_final_w"]


def kernel(**inputs):
    import numpy as np
    import concourse.bacc as bacc
    from concourse.bass_utils import run_bass_kernel_spmd

    nc = bacc.Bacc("TRN2", target_bir_lowering=False, num_devices=1)
    arrays, args = {}, []
    for name in _NAMES:
        a = np.ascontiguousarray(inputs[name])
        arrays["in_" + name] = a
        args.append(nc.dram_tensor("in_" + name, a.shape, mybir.dt.from_np(a.dtype), kind="ExternalInput").ap())
    args.append(nc.dram_tensor("acs_dram", (NT, HEADS, P), F32, kind="Internal").ap())
    args.append(nc.dram_tensor("out", (1, SEQ, D), F32, kind="ExternalOutput").ap())
    hymba_layer(nc, *args)
    r = run_bass_kernel_spmd(nc, [arrays], core_ids=[0])
    return r.results[0]["out"]
```

```python
from contextlib import ExitStack

import concourse.bass as bass
from concourse import mybir

ALU = mybir.AluOpType
ACT = mybir.ActivationFunctionType
AX = mybir.AxisListType
F32 = mybir.dt.float32
F32R = mybir.dt.float32r
BF16 = mybir.dt.bfloat16

P = 128
D = 1024
SEQ = 512
NT = SEQ // P
KD = D // P
HEADS = 16
PAIRS = HEADS // 2
HD = 64
GROUPS = 2
GH = HEADS // GROUPS
GW = D // GROUPS
NX = (D + 2 * GROUPS * P) // P
CONV = 4
MEM = 256
MB = MEM // P
MH = 4
MHD = D // MH
DFF = 2816
KF = DFF // P
FCONV = 3
EPS = 1e-6
NEG = -1e30

COL_Z = 0
COL_XBC = D
COL_DT = COL_XBC + NX * P
COL_Q = COL_DT + HEADS
COL_K = COL_Q + D
COL_V = COL_K + D

U_XBC = 0
U_DT = U_XBC + NX // 2
U_Z = U_DT + 1
U_V = U_Z + 4
U_QK = U_V + 4
U_MV = U_QK + PAIRS
U_MK = U_MV + 4
U_OUT = U_MK + 4
U_MQ = U_OUT + 8
U_MO = U_MQ + 4
U_UP = U_MO + 4
U_DOWN = U_UP + KF
DOWN_K = [KF % 4] + [4] * (KF // 4)
DOWN_AT = [sum(DOWN_K[:n]) for n in range(len(DOWN_K))]
U_ALL = U_DOWN + 2 * len(DOWN_K)

C_MIX, C_MEMKV, C_MEM, C_FFN, C_SBN = 0, 8, 16, 24, 32
C_CB, C_CW = 40, 52
C_FW, C_FB = 100, 232
C_ALL = C_FB + 2 * KF

START = [0, 128, 256, 256]
OFF = [0, 512, 896, 1152]
WID = [SEQ - s for s in START]
PACK = OFF[3] + WID[3]
CHUNK = [(0, 512), (512, 384), (896, 512)]
BLOCKS = [[0], [1], [2, 3]]
ORDER = [2, 1, 0]


class Steps:

    def __init__(self, engine, semaphore):
        self.engine, self.semaphore, self.n, self.base = engine, semaphore, 0, 0

    def did(self, instruction):
        self.n += 1
        return instruction.then_inc(self.semaphore, 1)

    def settle(self):
        self.engine.wait_ge(self.semaphore, self.base + self.n)

    def do(self, instruction):
        self.did(instruction)
        self.settle()

    def enter(self, i, per):
        self.before, self.per = self.n, per
        self.base = i * per

    def leave(self, times):
        assert self.n - self.before == self.per, (self.n - self.before, self.per)
        self.base = 0
        self.n = self.before + self.per * times


def hymba_layer(nc, x, mem, norm_mix_w, w_in, conv_ssd_w, conv_ssd_b, dt_bias, a_log, d_skip,
                ssd_norm_w, sb_norm_w, w_out, norm_mem_w, norm_memkv_w, w_mq, w_mk, w_mv, w_mo,
                norm_ffn_w, w_up, conv_ffn_w, conv_ffn_b, w_down, norm_final_w, acs_dram, out):
    with ExitStack() as ctx:
        def sb(name, shape, dt=F32, stack=ctx):
            return stack.enter_context(nc.sbuf_tensor(name, shape, dt))

        def sem(name):
            return ctx.enter_context(nc.semaphore(name))

        raw = sb("w_raw", [P, 2, 2048])
        w_hi = sb("w_hi", [P, 2, 2048], F32R)
        w_lo = sb("w_lo", [P, 2, 2048], F32R)
        a_hi = sb("a_hi", [P, KD, SEQ], F32R)
        a_lo = sb("a_lo", [P, KD, SEQ], F32R)
        ident = sb("ident", [P, P])
        ident_b = sb("ident_b", [P, P], BF16)
        neg_b = sb("neg_b", [P, 2 * P], BF16)
        ones = sb("ones", [P, P])
        head_sel = sb("head_sel", [P, HEADS - 2 + P])
        tri_u = sb("tri_u", [P, P])
        neg_tri = sb("neg_tri", [P, P], F32R)
        neg_one = sb("neg_one", [P, P], F32R)
        par = sb("par", [P, C_ALL])
        eps_t = sb("eps_t", [P, 1])
        ssq = sb("ssq", [P, 8])
        rms = sb("rms", [P, 8])
        rinv = sb("rinv", [P, 8])
        mem_ms = sb("mem_ms", [P, 3, MB])

        one = ExitStack()
        vx = sb("vx", [P, NX, SEQ], stack=one)
        xn = sb("xn", [P, NT, D], stack=one)
        zy = sb("zy", [P, NT, D], stack=one)
        small = one.enter_context(ExitStack())
        conv_acc = sb("conv_acc", [P, 2, SEQ], stack=small)
        b_nat = sb("b_nat", [P, NT, GROUPS, P], stack=small)
        cb_m = sb("cb_m", [P, GROUPS, P], stack=small)
        seg = sb("seg", [P, 2, HEADS, P], stack=small)
        xdt = sb("xdt", [P, 2, D + HD], stack=small)
        xdd = sb("xdd", [P, D], stack=small)
        xsk = sb("xsk", [P, D], stack=small)
        yt = sb("yt", [P, D], stack=small)
        carry = sb("carry", [P, D], stack=small)
        ssdn_w = sb("ssdn_w", [P, D], stack=small)
        head_b = sb("head_b", [P, 3, HEADS], stack=small)
        sc = sb("sc", [P, 12, NT * HEADS], stack=small)
        small.close()
        dtT, acsT = yt[0:HEADS, 0:SEQ], xsk[0:HEADS, 0:SEQ]
        q_hi = sb("q_hi", [P, 2, SEQ], F32R, one)
        q_lo = sb("q_lo", [P, 2, SEQ], F32R, one)
        k_hi = sb("k_hi", [P, SEQ], F32R, one)
        k_lo = sb("k_lo", [P, SEQ], F32R, one)
        v_hi = sb("v_hi", [P, NT, 3, HD], F32R, one)
        v_lo = sb("v_lo", [P, NT, 3, HD], F32R, one)
        s_hi = sb("s_hi", [P, 2, PACK], F32R, one)
        s_lo = sb("s_lo", [P, 2, PACK], F32R, one)
        p_hi = sb("p_hi", [P, PACK], F32R, one)
        p_lo = sb("p_lo", [P, PACK], F32R, one)
        work = sb("work", [P, 2, PACK], F32, one)
        one.close()
        mem_nat = vx[:, KD:, :].rearrange("p c s -> p (c s)").rearrange("p (b d) -> p b d", b=MB)
        v_nat = vx[:, 0:KD, :].rearrange("p c s -> p (c s)").rearrange("p (t d) -> p t d", t=NT)
        ysb = xn[:, :, :].rearrange("p t d -> p (t d)").rearrange("p (c s) -> p c s", c=KD)

        two = ExitStack()
        early = two.enter_context(ExitStack())
        m_hi = sb("m_hi", [P, KD, MEM], F32R, early)
        m_lo = sb("m_lo", [P, KD, MEM], F32R, early)
        x_blk = sb("x_blk", [P, 2, D], F32, early)
        early.close()
        late = two.enter_context(ExitStack())
        pt_hi = sb("pt_hi", [P, 2, MB, SEQ], F32R, late)
        pt_lo = sb("pt_lo", [P, 2, MB, SEQ], F32R, late)
        late.close()
        h2_hi = sb("h2_hi", [P, KD, SEQ], F32R, two)
        h2_lo = sb("h2_lo", [P, KD, SEQ], F32R, two)
        km_hi = sb("km_hi", [P, KD, MEM], F32R, two)
        vm_hi = sb("vm_hi", [P, MB, D], F32R, two)
        vm_lo = sb("vm_lo", [P, MB, D], F32R, two)
        b_hi = sb("b_hi", [P, KD, SEQ], F32R, two)
        with ExitStack() as same_place:
            sm_p = sb("sm_p", [P, MH, NT, MEM], F32, same_place)
        b_lo = sb("b_lo", [P, KD, SEQ], F32R, two)
        xT = sb("xT", [P, KD, SEQ], F32, two)
        two_top = two.enter_context(ExitStack())
        km_lo = sb("km_lo", [P, KD, MEM], F32R, two_top)
        with ExitStack() as same_place:
            inv_hl = sb("inv_hl", [P, 2, SEQ], F32R, same_place)
            head_rows = sb("head_rows", [P, D], F32R, same_place)
        sq = sb("sq", [P, 2, SEQ], F32, two_top)
        acc_s = sb("acc_s", [P, SEQ], F32, two_top)
        smx = sb("smx", [P, MH, 3, NT], F32, two_top)
        sb("gap", [P, 4 * (FCONV - 1 + SEQ) + 4 * SEQ - 2 * KD * MEM // 2 - 3 * SEQ - 3 * MH * NT], F32, two_top)
        r_row = sb("r_row", [P, SEQ], F32, two_top)
        two.close()


        three = ExitStack()
        ff_hi = sb("ff_hi", [P, KF, SEQ], F32R, three)
        ff_lo = sb("ff_lo", [P, KF, SEQ], F32R, three)
        three.enter_context(nc.sbuf_tensor("xT_stays", [P, KD, SEQ], F32))
        up = three.enter_context(ExitStack())
        u_pad = sb("u_pad", [P, 2, 2, FCONV - 1 + SEQ], F32, up)
        u_acc = sb("u_acc", [P, 2, 2, SEQ], F32, up)
        up.close()
        fin_w = sb("fin_w", [P, D], F32, three)
        Y_BUFS = 3
        y_out = sb("y_out", [P, Y_BUFS, D], F32, three)
        three.close()

        ps = ctx.enter_context(nc.psum_tensor("ps", [P, 8, SEQ], F32))

        S = {}
        for name in (
            "x_in0 x_in1 x_in2 x_in3 rows_in bcast_in mem_in raw_in0 raw_in1 fin_in "
            "acs_out seg_in0 seg_in1 xblk_in0 xblk_in1 y_sent0 y_sent "
            "consts consts_r w_hi_ok w_lo_ok w_used tile0_mm "
            "rms_ok x_scaled mem_rms mem_scaled par_tr par_ok x_tr h_hi_ok h_lo_ok "
            "conv_tap conv_ok conv_silu dtT_ok dt_tr dt_exp dt_ln dt_ok acs_mm "
            "acs_ok acsT_ok decay_ok nat_mm nat_ok xtr_mm xn_even xn_odd cb_mm cb_ok seg_ok seg_exp "
            "m_ok xd_ok diag_mm state_mm y_ok carry_ok y_gated ssd_rms ssd_ok "
            "q_hi_ok q_ok k_hi_ok k_ok v_hi_ok v_ok pad_ok z_mm ln_ok soft_ok cs_mm "
            "prob_ok p_ok av_mm o_ok ytr_mm yh_ok yl_ok mtr_mm mh_ok ml_ok "
            "mk_hi_ok mk_ok mv_mm mv_hi_ok mv_ok sb_sq sb_mm sb_rms sb_inv head_rows_ok sb_bc sb_y sb_hi_ok sb_ok "
            "res_tr res_ok res_sum res_sq res_hi res_lo row_mm row_rms row_ok "
            "mq_f mq_hi_ok mq_ok sm_mm sm_max sm_exp sm_div pt_mm pt_hi_ok pt_ok o_mm "
            "mo_hi_ok mo_ok up_pad up_tap up_conv up_silu up_f up_hi_ok up_ok "
            "down_mm fin_sq fin_ms fin_rms fin_y act_step dve_step pool_step"
        ).split():
            S[name] = sem(name)
        s = S
        raw_in = [s["raw_in0"], s["raw_in1"]]
        seg_in = [s["seg_in0"], s["seg_in1"]]
        xblk_in = [s["xblk_in0"], s["xblk_in1"]]
        x_in = [s[f"x_in{t}"] for t in range(NT)]


        DVE_SC = ["v", "u", "w", "ln", "d", "z", "dt", "a", "acs", "e", "dec", "cd"]

        def col(name):
            return sc[:, DVE_SC.index(name), :]

        def heads_of(name, c, g, width):
            a = col(name)[:, c * HEADS + g * GH:c * HEADS + (g + 1) * GH]
            return a.unsqueeze(2).to_broadcast([P, GH, width])

        def all_heads(name, c, width):
            return col(name)[:, c * HEADS:(c + 1) * HEADS].unsqueeze(2).to_broadcast([P, HEADS, width])

        def k_of(half):
            return slice(4 * half, 4 * half + 4)

        win = w_in[0].rearrange("(k p) n -> p k n", p=P)
        block = ctx.enter_context(nc.Block())

        def tile_done(engine, u, m):
            if m == 0:
                engine.wait_ge(s["tile0_mm"], u + 1)
            else:
                engine.wait_ge(s["w_used"], u + 3)

        def nat_done(engine, h, t):
            if t < NT - 1:
                engine.wait_ge(s["nat_mm"], (NT - 1) * h + t + 1)
            else:
                engine.wait_ge(s["w_used"], U_Z + 2 * h + 1 + 3)

        def mv_done(engine, h, b):
            if b == 0:
                engine.wait_ge(s["mv_mm"], h + 1)
            else:
                engine.wait_ge(s["w_used"], U_MV + 2 * h + 1 + 3)

        def down_done(engine, half, t):
            if t < NT - 1:
                engine.wait_ge(s["down_mm"], (NT - 1) * half + t + 1)
            else:
                engine.wait_ge(s["w_used"], U_DOWN + (half + 1) * len(DOWN_K) - 1 + 3)

        def z_bank(e, j):
            return 2 + 3 * e + j

        def sm_bank(h, t):
            return (2 + 2 * h + t // 2) % 8

        def mq_bank(h, m):
            return (4 if h == 1 else 0) + m

        def pt_bank(h, b):
            return 2 + 2 * (h % 2) + b

        def v_pair(p):
            v4 = v_nat.rearrange("p t (h d) -> p t h d", d=HD)
            return v4[:, :, bass.ds(2 * p, 2), :]

        def conv_w_col(tap, tile):
            return par[:, bass.ds(C_CW + tap * NX + tile, 1)]

        def ffn_w_col(tap, m, tile):
            return par[:, bass.ds(C_FW + tap * 2 * KF + m * KF + tile, 1)]

        MEM_BANKS = [0, 2, 3, 4]
        Y_BANKS = [0, 1, 7]

        SB_ORDER = [4, 5, 6, 7, 0, 1, 2, 3]

        @block.sync
        def _(sp):
            sp.sem_inc(s["w_lo_ok"], 2)

            def unit(u, parity, parts):
                sp.wait_ge(s["w_lo_ok"], u + 1)
                for dst, src in parts:
                    sp.dma_start(dst, src).then_inc(raw_in[parity], 16)

            def t_parts(parity, w, c0, rows=0, width=256):
                dst = raw[:, parity].rearrange("p (k n) -> p k n", k=KD)[:, :, 0:width]
                return [(dst[:, k_of(h)], w[:, rows + 4 * h:rows + 4 * h + 4, bass.ds(c0, width)])
                        for h in range(2)]

            def n_parts(parity, w, k0, kn, c0):
                dst = raw[:, parity].rearrange("p (k n) -> p k n", k=4)
                half = kn // 2
                return [(dst[:, h * half:(h + 1) * half], w[:, k0 + h * half:k0 + (h + 1) * half, c0:c0 + 512])
                        for h in range(2)]

            def two_tiles(parity, w, c0, c1):
                dst = raw[:, parity].rearrange("p (k m n) -> p k m n", k=KD, m=2)
                return [(dst[:, :, m], w[:, :, bass.ds(c, P)]) for m, c in enumerate((c0, c1))]

            for t in range(0, NT, 2):
                sp.dma_start(xn[:, t, :], x[0, t * P:(t + 1) * P, :]).then_inc(x_in[t], 16)
            unit(0, 0, t_parts(0, win, COL_XBC))
            rows = zy
            for r0, w in ((C_MIX, norm_mix_w), (C_MEMKV, norm_memkv_w), (C_MEM, norm_mem_w), (C_FFN, norm_ffn_w),
                          (C_SBN, sb_norm_w), (C_CB, conv_ssd_b)):
                v = w.rearrange("o (k p) -> (o k) p", p=P)
                sp.dma_start(rows[r0:r0 + v.shape[0], 0, 0:P], v).then_inc(s["rows_in"], 16)
            cw = conv_ssd_w[0].rearrange("t (k p) -> (t k) p", p=P)
            sp.dma_start(rows[C_CW:C_CW + CONV * NX, 0, 0:P], cw).then_inc(s["rows_in"], 16)
            fw = conv_ffn_w[0].rearrange("t (k p) -> (t k) p", p=P)
            fb = conv_ffn_b.rearrange("o (k p) -> (o k) p", p=P)
            sp.dma_start(rows[0:4 * KF, 1, 0:P], fw[0:4 * KF]).then_inc(s["rows_in"], 16)
            sp.dma_start(rows[0:2 * KF, 2, 0:P], fw[4 * KF:6 * KF]).then_inc(s["rows_in"], 16)
            sp.dma_start(rows[2 * KF:4 * KF, 2, 0:P], fb).then_inc(s["rows_in"], 16)
            unit(1, 1, t_parts(1, win, COL_XBC + 256))
            with sp.Fori(1, NX // 4) as i:
                for j in range(2):
                    unit(2 * i + j, j, t_parts(j, win, COL_XBC + 512 * i + 256 * j))
            unit(U_DT, U_DT % 2, t_parts(U_DT % 2, win, COL_DT, width=HEADS))

            def seg_load(c):
                if c >= 2:
                    sp.wait_ge(s["diag_mm"], 2 * (c - 1))
                sp.dma_start(seg[:, c % 2], acs_dram[c:c + 1].to_broadcast([P, HEADS, P])
                             ).then_inc(seg_in[c % 2], 16)

            for n in range(8):
                u = U_Z + n
                base, half, kh = (COL_Z if n < 4 else COL_V), (n % 4) // 2, n % 2
                unit(u, u % 2, n_parts(u % 2, win, 4 * kh, 4, base + 512 * half))
                if n == 2:
                    sp.wait_ge(s["acsT_ok"], 1)
                    sp.dma_start(acs_dram.rearrange("c h l -> h c l"),
                                 acsT.rearrange("h (c l) -> h c l", c=NT)).then_inc(s["acs_out"], 16)
                if n == 3:
                    sp.wait_ge(s["acs_out"], 16)
                    seg_load(0)
                    seg_load(1)
                if n == 7:
                    seg_load(2)
            unit(U_QK, U_QK % 2, two_tiles(U_QK % 2, win, COL_Q, COL_K))
            seg_load(3)
            unit(U_QK + 1, (U_QK + 1) % 2, two_tiles((U_QK + 1) % 2, win, COL_Q + P, COL_K + P))
            sp.wait_ge(s["y_ok"], 2 * NT)
            sp.dma_start(mem_nat, mem[0].rearrange("(b p) d -> p b d", p=P)).then_inc(s["mem_in"], 16)
            with sp.Fori(0, 3) as i:
                for j in range(2):
                    u0 = U_QK + 2 + j
                    unit(u0 + 2 * i, u0 % 2, two_tiles(u0 % 2, win, COL_Q + (2 + j) * P + 2 * P * i,
                                                       COL_K + (2 + j) * P + 2 * P * i))
            wmk = w_mk[0].rearrange("(k p) n -> p k n", p=P)
            wmv = w_mv[0].rearrange("(k p) n -> p k n", p=P)

            def input_block(n):
                if n == 0:
                    sp.wait_ge(s["mtr_mm"], 4)
                if n >= 2:
                    sp.wait_ge(s["res_tr"], 2 * (n - 1))
                sp.dma_start(x_blk[:, n % 2], x[0, n * P:(n + 1) * P, :]).then_inc(xblk_in[n % 2], 16)

            for n in range(4):
                u = U_MV + n
                unit(u, u % 2, n_parts(u % 2, wmv, 4 * (n % 2), 4, 512 * (n // 2)))
            input_block(0)
            input_block(1)
            for n in range(4):
                u = U_MK + n
                unit(u, u % 2, t_parts(u % 2, wmk, 256 * n))
                if n >= 2:
                    input_block(n)
            wout = w_out[0].rearrange("(k p) n -> p k n", p=P)
            with sp.Fori(0, 4) as i:
                for j in range(2):
                    u0 = U_OUT + j
                    unit(u0 + 2 * i, u0 % 2, t_parts(u0 % 2, wout, 256 * i, rows=KD * j))
            for first, w in ((U_MQ, w_mq), (U_MO, w_mo)):
                wv = w[0].rearrange("(k p) n -> p k n", p=P)
                with sp.Fori(0, 2) as i:
                    for j in range(2):
                        u0 = first + j
                        unit(u0 + 2 * i, u0 % 2, t_parts(u0 % 2, wv, 512 * i + 256 * j))
            wup = w_up[0].rearrange("(k p) n -> p k n", p=P)
            with sp.Fori(0, KF // 2) as i:
                for j in range(2):
                    u0 = U_UP + j
                    unit(u0 + 2 * i, u0 % 2, two_tiles(u0 % 2, wup, 2 * P * i + P * j, DFF + 2 * P * i + P * j))
            wdn = w_down[0].rearrange("(k p) n -> p k n", p=P)
            for half in range(2):
                for n, kn in enumerate(DOWN_K):
                    u = U_DOWN + half * len(DOWN_K) + n
                    unit(u, u % 2, n_parts(u % 2, wdn, DOWN_AT[n], kn, 512 * half))
            sp.wait_ge(s["up_ok"], KF + 2)
            sp.dma_start(fin_w[:], norm_final_w.unsqueeze(0).to_broadcast([P, D])).then_inc(s["fin_in"], 16)
            for t in range(NT):
                sp.wait_ge(s["fin_y"], 2 * t + 2)
                sp.dma_start(out[0, t * P:(t + 1) * P], y_out[:, t % Y_BUFS]
                             ).then_inc(s["y_sent" if t else "y_sent0"], 16)
            sp.wait_ge(s["y_sent0"], 16)
            sp.wait_ge(s["y_sent"], 16 * (NT - 1))

        @block.gpsimd
        def _(pool):
            step = Steps(pool, s["pool_step"])
            tmp = conv_acc

            def select(out_ap, pattern, fill, compare, multiplier, base=0):
                return pool.affine_select(out=out_ap, in_=out_ap, compare_op=compare, fill=fill, base=base,
                                          pattern=pattern, channel_multiplier=multiplier)

            step.did(pool.memset(ident[:], 0.0))
            pool.memset(eps_t[:], EPS).then_inc(s["consts"], 1)
            step.did(pool.memset(tri_u[:], 1.0))
            step.did(pool.memset(tmp[:, 0, 0:P], -1.0))
            step.did(pool.memset(tmp[:, 1, 0:2 * P], 0.0))
            step.did(pool.memset(head_sel[:], 0.0))
            step.settle()
            select(ident[:], [[-1, P]], 1.0, ALU.not_equal, 1).then_inc(s["consts"], 1)
            select(tri_u[:], [[1, P]], 0.0, ALU.is_ge, -1).then_inc(s["consts"], 1)
            select(tmp[:, 0, 0:P], [[-1, P]], 0.0, ALU.is_ge, 1).then_inc(s["consts"], 1)
            step.do(pool.memset(tmp[:, 1, 0:P], NEG))
            select(tmp[:, 1, P:2 * P], [[1, P]], NEG, ALU.is_gt, -1).then_inc(s["consts"], 1)
            pool.memset(tmp[:, 0, P:2 * P], -1.0).then_inc(s["consts"], 1)
            pool.wait_ge(s["consts"], 6)
            pool.memset(head_sel[0:HD, HEADS - 2:HEADS - 1], 1.0).then_inc(s["consts"], 1)
            pool.wait_ge(s["consts"], 7)
            pool.memset(head_sel[HD:P, HEADS - 1:HEADS], 1.0).then_inc(s["consts"], 1)
            pool.wait_ge(s["consts"], 8)
            pool.memset(ones[:], 1.0).then_inc(s["consts"], 1)
            pool.memset(xdt[:, :, D:D + HD], 0.0).then_inc(s["consts"], 1)

            def lo(u, parity, cycle):
                pool.wait_ge(raw_in[parity], 32 * cycle)
                pool.wait_ge(s["w_hi_ok"], u + 1)
                pool.wait_ge(s["w_used"], u + 1)
                pool.tensor_tensor(w_lo[:, parity], raw[:, parity], w_hi[:, parity].bitcast(F32),
                                   ALU.subtract).then_inc(s["w_lo_ok"], 1)

            def lo_at(u):
                lo(u, u % 2, u // 2 + 1)

            def ssd_inputs(c):
                xc = xn[:, c].rearrange("p (h d) -> p h d", h=HEADS)
                xd = xdt[:, c % 2, 0:D].rearrange("p (h d) -> p h d", h=HEADS)
                if c == 0:
                    pool.wait_ge(s["xn_even"], 4)
                    pool.wait_ge(s["xn_odd"], 6)
                    pool.wait_ge(s["acs_out"], 16)
                    pool.wait_ge(s["decay_ok"], 3)
                    pool.wait_ge(s["bcast_in"], 64)
                if c >= 2:
                    pool.wait_ge(s["diag_mm"], 2 * (c - 1))
                pool.tensor_tensor(xd, xc, all_heads("dt", c, HD), ALU.mult).then_inc(s["xd_ok"], 1)
                if c >= 1:
                    pool.wait_ge(s["y_ok"], 2 * c)
                pool.tensor_tensor(xsk[:].rearrange("p (h d) -> p h d", h=HEADS), xc,
                                   head_b[:, 2].unsqueeze(2).to_broadcast([P, HEADS, HD]),
                                   ALU.mult).then_inc(s["xd_ok"], 1)
                if c < NT - 1:
                    pool.wait_ge(s["xd_ok"], 3 * c + 1)
                    if c >= 1:
                        pool.wait_ge(s["state_mm"], 2 * c)
                    pool.tensor_tensor(xdd[:].rearrange("p (h d) -> p h d", h=HEADS), xd,
                                       all_heads("dec", c, HD), ALU.mult).then_inc(s["xd_ok"], 1)

            with pool.Fori(0, U_DT // 2) as i:
                for j in range(2):
                    lo(2 * i + j, j, i + 1)
            pool.wait_ge(raw_in[U_DT % 2], 32 * (U_DT // 2 + 1))
            pool.wait_ge(s["w_hi_ok"], U_DT + 1)
            pool.wait_ge(s["w_used"], U_DT + 1)
            dt_cols = [t[:, U_DT % 2].rearrange("p (k n) -> p k n", k=KD)[:, :, 0:HEADS] for t in (w_lo, raw, w_hi)]
            pool.tensor_tensor(dt_cols[0], dt_cols[1], dt_cols[2].bitcast(F32), ALU.subtract
                               ).then_inc(s["w_lo_ok"], 1)
            for u in range(U_DT + 1, 10):
                lo_at(u)
            for u in range(10, 14):
                lo_at(u)
                ssd_inputs(u - 10)
            lo_at(14)
            lo_at(15)
            pool.wait_ge(s["ssd_rms"], 1)
            pool.wait_ge(s["w_lo_ok"], 16 + 2)
            for n, t in enumerate((q_hi, q_lo)):
                if n:
                    pool.wait_ge(s["pad_ok"], 2)
                pool.memset(t[HD:P, 0, :].bitcast(F32), 0.0).then_inc(s["pad_ok"], 1)
                pool.wait_ge(s["pad_ok"], 2 * n + 1)
                pool.memset(t[0:HD, 1, :].bitcast(F32), 0.0).then_inc(s["pad_ok"], 1)
            pool.wait_ge(s["pad_ok"], 4)
            for t in (v_hi, v_lo):
                pool.memset(t[:, :, 1, :].bitcast(F32), 0.0).then_inc(s["pad_ok"], 1)

            def pair(p, u0, i):
                pool.wait_ge(s["v_hi_ok"], p + 1)
                pool.tensor_tensor(v_lo[:, :, 0::2, :], v_pair(p), v_hi[:, :, 0::2, :].bitcast(F32),
                                   ALU.subtract).then_inc(s["v_ok"], 1)
                if u0 is not None:
                    lo(u0 + 2 * i, u0 % 2, u0 // 2 + 1 + i)

            lo_at(16)
            pair(0, 17, 0)
            with pool.Fori(0, 3) as i:
                for j in range(2):
                    pair(1 + j + 2 * i, 18 + j, i)
            pair(7, 24, 0)
            pool.wait_ge(s["p_ok"], 3 * HEADS + 6)
            step.do(pool.memset(head_rows[:].bitcast(F32), 1.0))
            step.do(select(head_rows[:], [[1, D]], 0.0, ALU.is_ge, -HD))
            select(head_rows[:], [[-1, D]], 0.0, ALU.is_ge, HD, HD - 1).then_inc(s["head_rows_ok"], 1)
            assert U_ALL % 2 == 1
            with pool.Fori(0, (U_ALL - 25) // 2) as i:
                for j in range(2):
                    u0 = 25 + j
                    lo(u0 + 2 * i, u0 % 2, u0 // 2 + 1 + i)

        @block.scalar
        def _(act):
            step = Steps(act, s["act_step"])

            def copy_scaled(dst, src, scale=1.0):
                return act.activation(dst, src, ACT.Copy, scale=scale)

            def hi(u, parity, cycle):
                act.wait_ge(raw_in[parity], 32 * cycle)
                act.wait_ge(s["w_used"], u + 1)
                act.copy(w_hi[:, parity], raw[:, parity]).then_inc(s["w_hi_ok"], 1)

            def hi_at(u):
                hi(u, u % 2, u // 2 + 1)

            for t in range(1, NT, 2):
                act.dma_start(xn[:, t, :], x[0, t * P:(t + 1) * P, :]).then_inc(x_in[t], 16)

            act.wait_ge(s["consts"], 1)
            step.did(act.activation(mem_ms[:, 0, 0:1], eps_t[:], ACT.Sqrt))
            for t in range(NT):
                act.wait_ge(x_in[t], 16)
                step.do(act.activation(vx[:, 2 * t:2 * t + 2, :].rearrange("p a b -> p (a b)"), xn[:, t],
                                       ACT.Square, accum_out=ssq[:, t:t + 1]))
                act.activation(rms[:, t:t + 1], ssq[:, t:t + 1], ACT.Sqrt, scale=1.0 / D, bias=eps_t[:]
                               ).then_inc(s["rms_ok"], 1)
            act.wait_ge(s["consts"], 10)
            act.copy(neg_tri[:], conv_acc[:, 0, 0:P]).then_inc(s["consts_r"], 1)
            act.copy(neg_one[:], conv_acc[:, 0, P:2 * P]).then_inc(s["consts_r"], 1)
            act.copy(neg_b[:], conv_acc[:, 1, 0:2 * P]).then_inc(s["consts_r"], 1)
            act.copy(ident_b[:], ident[:]).then_inc(s["consts_r"], 1)
            act.wait_ge(s["par_tr"], 1)
            act.copy(par[:], ps[:, 7, 0:C_ALL]).then_inc(s["par_ok"], 1)
            act.wait_ge(s["par_ok"], 1)
            for c in range(KD):
                act.wait_ge(s["x_tr"], c + 1)
                copy_scaled(a_hi[:, c], ps[:, c], par[:, C_MIX + c:C_MIX + c + 1]).then_inc(s["h_hi_ok"], 1)
            for n, w in enumerate((dt_bias, a_log, d_skip)):
                act.dma_start(head_b[:, n], w.to_broadcast([P, HEADS])).then_inc(s["bcast_in"], 16)
            act.dma_start(ssdn_w[:], ssd_norm_w.to_broadcast([P, D])).then_inc(s["bcast_in"], 16)

            hi_at(1)
            act.sem_inc(s["conv_silu"], 2)
            with act.Fori(0, NX // 4) as i:
                def conv_act(j):
                    act.wait_ge(s["conv_ok"], 4 * i + j + 1 + 4)
                    act.activation(vx[:, bass.ds(4 * i + j, 1), :], conv_acc[:, j % 2:j % 2 + 1, :], ACT.Silu
                                   ).then_inc(s["conv_silu"], 1)

                for j in range(4):
                    n = 4 * i + j
                    tile_done(act, 2 * i + j // 2, j % 2)
                    if j % 2 == 1:
                        u0 = 2 + j // 2
                        hi(u0 + 2 * i, u0 % 2, u0 // 2 + 1 + i)
                    act.wait_ge(s["conv_silu"], n + 1)
                    act.activation(conv_acc[:, j % 2], ps[:, j], ACT.Identity, scale=conv_w_col(CONV - 1, n),
                                   bias=par[:, bass.ds(C_CB + n, 1)]).then_inc(s["conv_tap"], 1)
                    if j:
                        conv_act(j - 1)
                conv_act(3)
            act.wait_ge(s["dt_ok"], 1)
            step.do(act.activation(col("z"), col("v"), ACT.Abs))
            act.activation(col("u"), col("z"), ACT.Exp, scale=-1.0).then_inc(s["dt_exp"], 1)
            act.wait_ge(s["bcast_in"], 64)
            act.activation(head_b[:, 1], head_b[:, 1], ACT.Exp).then_inc(s["dt_exp"], 1)
            act.wait_ge(s["dt_ok"], 2)
            act.activation(col("ln"), col("w"), ACT.Ln).then_inc(s["dt_ln"], 1)
            hi_at(8)
            act.wait_ge(s["acs_ok"], 3)
            act.activation(col("e"), col("acs"), ACT.Exp).then_inc(s["decay_ok"], 1)
            act.activation(col("dec"), col("dec"), ACT.Exp).then_inc(s["decay_ok"], 1)
            act.activation(col("cd"), col("cd"), ACT.Exp).then_inc(s["decay_ok"], 1)

            def nat_evac(h):
                for t in range(NT):
                    nat_done(act, h, t)
                    if h < 2:
                        act.activation(zy[:, t, 512 * h:512 * h + 512], ps[:, t], ACT.Silu).then_inc(s["nat_ok"], 1)
                    else:
                        act.copy(v_nat[:, t, 512 * (h - 2):512 * (h - 1)], ps[:, t]).then_inc(s["nat_ok"], 1)

            def seg_exp(c):
                act.wait_ge(s["seg_ok"], HEADS * (c + 1))
                act.activation(seg[:, c % 2], seg[:, c % 2], ACT.Exp).then_inc(s["seg_exp"], 1)

            def gated_squares(c):
                for g in range(GROUPS):
                    act.wait_ge(s["y_gated"], 2 * c + g + 1)
                    step.did(act.activation(conv_acc[:, 0], zy[:, c, g * GW:(g + 1) * GW], ACT.Square,
                                            accum_out=ssq[:, 2 * c + g:2 * c + g + 1]))
                    step.settle()

            hi_at(9)
            nat_evac(0)
            hi_at(10)
            for c in range(0, KD, 2):
                act.wait_ge(s["xtr_mm"], c + 1)
                act.copy(xn[:, :, c * P:(c + 1) * P], ps[:, 4 + c % 4].rearrange("p (t n) -> p t n", t=NT)
                         ).then_inc(s["xn_even"], 1)
            seg_exp(0)
            hi_at(11)
            nat_evac(1)
            seg_exp(1)
            hi_at(12)
            gated_squares(0)
            seg_exp(2)
            hi_at(13)
            nat_evac(2)
            gated_squares(1)
            seg_exp(3)
            hi_at(14)
            gated_squares(2)
            hi_at(15)
            nat_evac(3)
            gated_squares(3)
            act.activation(rms[:, 0:8], ssq[:, 0:8], ACT.Sqrt, scale=1.0 / GW, bias=eps_t[:]
                           ).then_inc(s["ssd_rms"], 1)
            hi_at(16)

            def q_evac(p):
                tile_done(act, U_QK + p, 0)
                if isinstance(p, int) and p == 0:
                    act.wait_ge(s["pad_ok"], 6)
                act.wait_ge(s["z_mm"], 6 * p + 6)
                copy_scaled(q_hi[0:HD, 0], ps[0:HD, 0], HD ** -0.5).then_inc(s["q_hi_ok"], 1)
                copy_scaled(q_hi[HD:P, 1], ps[HD:P, 0], HD ** -0.5).then_inc(s["q_hi_ok"], 1)

            def k_evac(p):
                tile_done(act, U_QK + p, 1)
                act.copy(k_hi[:], ps[:, 1]).then_inc(s["k_hi_ok"], 1)

            def soft_exp(p, e):
                n = 2 * p + e
                for c, j in enumerate(ORDER):
                    o, w = CHUNK[j]
                    act.wait_ge(s["z_mm"], 3 * n + c + 1 + 6)
                    act.wait_ge(s["p_ok"], 3 * n + c + 1)
                    step.did(act.activation(work[:, e, o:o + w], ps[:, z_bank(e, j), 0:w], ACT.Abs))
                step.settle()
                for j in ORDER:
                    o, w = CHUNK[j]
                    step.did(act.activation(work[:, e, o:o + w], work[:, e, o:o + w], ACT.Exp, scale=-1.0))

            def soft_ln(e):
                for j in ORDER:
                    o, w = CHUNK[j]
                    act.activation(work[:, e, o:o + w], work[:, e, o:o + w], ACT.Ln, bias=1.0
                                   ).then_inc(s["ln_ok"], 1)

            def probs(p, e):
                n = 2 * p + e
                for c, j in enumerate(ORDER):
                    o, w = CHUNK[j]
                    act.wait_ge(s["cs_mm"], 3 * n + c + 1)
                    act.activation(work[:, e, o:o + w], ps[:, z_bank(e, j), 0:w], ACT.Exp).then_inc(s["prob_ok"], 1)

            def o_evac(p):
                act.wait_ge(s["av_mm"], 2 * p + 2)
                act.copy(ysb[:, bass.ds(p, 1), :], ps[:, 1:2, :]).then_inc(s["o_ok"], 1)

            def v_round(p):
                act.wait_ge(s["av_mm"], 2 * p)
                act.copy(v_hi[:, :, 0::2, :], v_pair(p)).then_inc(s["v_hi_ok"], 1)

            def pair(p, u0=None, i=0, first=False):
                last = u0 is None
                if not first:
                    probs(p - 1, 1)
                soft_exp(p, 0)
                if last:
                    step.settle()
                    soft_ln(0)
                soft_exp(p, 1)
                if not first:
                    o_evac(p - 1)
                step.settle()
                if not last:
                    soft_ln(0)
                soft_ln(1)
                if not first:
                    v_round(p)
                if not last:
                    q_evac(p + 1)
                    hi(u0 + 2 * i, u0 % 2, u0 // 2 + 1 + i)
                    k_evac(p + 1)
                if first:
                    memory_rms()
                probs(p, 0)

            def memory_rms():
                act.wait_ge(s["mem_in"], 16)
                for b in range(MB):
                    step.do(act.activation(p_hi[:, 0:D], mem_nat[:, b], ACT.Square,
                                           accum_out=mem_ms[:, 0, b:b + 1]))
                act.activation(mem_ms[:, 1], mem_ms[:, 0], ACT.Sqrt, scale=1.0 / D, bias=eps_t[:]
                               ).then_inc(s["mem_rms"], 1)

            act.sem_inc(s["prob_ok"], 6)
            q_evac(0)
            k_evac(0)
            act.wait_ge(s["nat_ok"], 16)
            act.copy(v_hi[:, :, 0::2, :], v_pair(0)).then_inc(s["v_hi_ok"], 1)
            pair(0, 17, first=True)
            with act.Fori(0, 3) as i:
                step.enter(i, 24)
                for j in range(2):
                    pair(1 + j + 2 * i, 18 + j, i)
                step.leave(3)
            hi_at(24)
            pair(7)
            probs(7, 1)

            act.wait_ge(s["v_ok"], 8)
            for b in range(4):
                act.wait_ge(s["mtr_mm"], b + 1)
                for c in (2 * b, 2 * b + 1):
                    copy_scaled(m_hi[:, c], ps[:, MEM_BANKS[b], (c % 2) * MEM:(c % 2 + 1) * MEM],
                                par[:, C_MEMKV + c:C_MEMKV + c + 1]).then_inc(s["mh_ok"], 1)
            o_evac(7)

            def y_round(c):
                act.wait_ge(s["ytr_mm"], c + 1)
                act.copy(a_hi[:, c], ps[:, Y_BANKS[c % 3]]).then_inc(s["yh_ok"], 1)

            def sb_square(n):
                if n >= 2:
                    act.wait_ge(s["sb_mm"], n - 1)
                act.activation(sq[:, n % 2], ysb[:, SB_ORDER[n]], ACT.Square).then_inc(s["sb_sq"], 1)

            def sb_round(n):
                act.wait_ge(s["sb_y"], n + 1)
                act.copy(b_hi[:, SB_ORDER[n]], ysb[:, SB_ORDER[n]]).then_inc(s["sb_hi_ok"], 1)

            act.wait_ge(s["o_ok"], 8)
            sb_square(0)
            sb_square(1)
            hi_at(U_MV + 2)
            y_round(0)
            y_round(1)
            for n in range(2, KD):
                sb_square(n)
            act.wait_ge(s["sb_mm"], KD)
            act.activation(r_row[:], ps[:, 6], ACT.Sqrt, scale=1.0 / HD, bias=eps_t[:]).then_inc(s["sb_rms"], 1)
            y_round(2)
            y_round(3)
            act.wait_ge(s["sb_inv"], 1)
            act.copy(inv_hl[:, 0], r_row[:]).then_inc(s["sb_rms"], 1)
            for h in range(2):
                hi_at(U_MV + 2 * h + 3)
                if h == 0:
                    for c in range(4, KD):
                        y_round(c)
                for b in range(MB):
                    mv_done(act, h, b)
                    act.copy(vm_hi[:, b, 512 * h:512 * h + 512], ps[:, 2 + 2 * h + b]).then_inc(s["mv_hi_ok"], 1)
                if h == 0:
                    hi_at(U_MV + 4)
                    sb_round(0)
                    sb_round(1)
            sb_round(2)
            sb_round(3)
            act.wait_ge(s["sb_ok"], 4)
            for n in range(4):
                for m in range(2):
                    tile_done(act, U_MK + n, m)
                    act.copy(km_hi[:, 2 * n + m], ps[:, m, 0:MEM]).then_inc(s["mk_hi_ok"], 1)
                hi_at(U_MK + n + 2)
                for q in range(2):
                    act.wait_ge(s["res_tr"], 2 * n + q + 1)
                    act.copy(xT[:, 4 * q:4 * q + 4, n * P:(n + 1) * P],
                             ps[:, 6 + q].rearrange("p (c n) -> p c n", c=4)).then_inc(s["res_ok"], 1)
                sb_round(4 + n)

            def residual(n, n8, m, c_gain, dst):
                act.wait_ge(s["res_sum"], n8 + 3)
                act.wait_ge(s["res_lo"], n8 + 1)
                act.activation(sq[:, m:m + 1], xT[:, bass.ds(n, 1)], ACT.Square).then_inc(s["res_sq"], 1)
                copy_scaled(dst[:, bass.ds(n, 1)], xT[:, bass.ds(n, 1)], par[:, bass.ds(c_gain + n, 1)]
                            ).then_inc(s["res_hi"], 1)

            def row_root(n):
                act.wait_ge(s["row_mm"], n + 1)
                act.activation(r_row[:], ps[:, 6], ACT.Sqrt, scale=1.0 / D, bias=eps_t[:]).then_inc(s["row_rms"], 1)

            with act.Fori(0, 4) as i:
                hi(U_OUT + 2 + 2 * i, U_OUT % 2, (U_OUT + 2) // 2 + 1 + i)
                for m in range(2):
                    residual(2 * i + m, 2 * i + m, m, C_MEM, h2_hi)
                hi(U_OUT + 3 + 2 * i, (U_OUT + 1) % 2, (U_OUT + 3) // 2 + 1 + i)
            row_root(0)
            def sm_exps(h):
                for t in range(NT):
                    act.wait_ge(s["sm_max"], 2 * h + t // 2 + 1)
                    act.activation(sm_p[:, h, t], ps[:, sm_bank(h, t), (t % 2) * MEM:(t % 2 + 1) * MEM], ACT.Exp,
                                   bias=smx[:, h, 0, t:t + 1], accum_out=smx[:, h, 1, t:t + 1]
                                   ).then_inc(s["sm_exp"], 1)

            def pt_round(h):
                for b in range(MB):
                    act.wait_ge(s["pt_mm"], 2 * h + b + 1)
                    if h >= 2:
                        act.wait_ge(s["o_mm"], 2 * (h - 1))
                    act.copy(pt_hi[:, h % 2, b], ps[:, pt_bank(h, b)]).then_inc(s["pt_hi_ok"], 1)

            def mo_round(h):
                for m in range(2):
                    act.wait_ge(s["o_mm"], 2 * h + m + 1)
                    act.copy(b_hi[:, 2 * h + m], ps[:, 6 + m]).then_inc(s["mo_hi_ok"], 1)

            for h in range(MH):
                if h >= 2:
                    sm_exps(h - 2)
                for m in range(2):
                    c = 2 * h + m
                    act.wait_ge(s["mq_f"], c + 1)
                    act.copy(a_hi[:, c], sq[:, m]).then_inc(s["mq_hi_ok"], 1)
                hi_at(U_MQ + h + 2)
            sm_exps(2)
            pt_round(0)
            sm_exps(3)
            for h in range(MH):
                if h < MH - 1:
                    pt_round(h + 1)
                mo_round(h)
            with act.Fori(0, 2) as i:
                for j in range(2):
                    for m in range(2):
                        n = 4 * i + 2 * j + m
                        residual(n, KD + n, m, C_FFN, a_hi)
                    u0 = U_MO + j + 2
                    hi(u0 + 2 * i, u0 % 2, u0 // 2 + 1 + i)
            row_root(1)

            act.sem_inc(s["up_tap"], 4)
            with act.Fori(0, KF // 2) as i:
                for j in range(2):
                    n = 2 * i + j
                    u0 = U_UP + j + 2
                    hi(u0 + 2 * i, u0 % 2, u0 // 2 + 1 + i)
                    for m in range(2):
                        act.wait_ge(s["up_pad"], 2 * n + m + 1 + 4)
                        act.wait_ge(s["up_ok"], n + 1)
                        act.activation(u_acc[:, j, m], u_pad[:, j, m, FCONV - 1:], ACT.Identity,
                                       scale=ffn_w_col(FCONV - 1, m, n),
                                       bias=par[:, bass.ds(C_FB + m * KF + n, 1)]).then_inc(s["up_tap"], 1)
                    act.wait_ge(s["up_conv"], 2 * n + 1)
                    act.activation(u_acc[:, j, 0], u_acc[:, j, 0], ACT.Silu).then_inc(s["up_silu"], 1)
                    act.wait_ge(s["up_f"], n + 1)
                    act.copy(ff_hi[:, bass.ds(n, 1)], u_acc[:, j, 0:1]).then_inc(s["up_hi_ok"], 1)
            for half in range(2):
                for n in range(len(DOWN_K)):
                    u = U_DOWN + half * len(DOWN_K) + n + 2
                    if u < U_ALL:
                        hi_at(u)
                for t in range(NT):
                    k = NT * half + t
                    down_done(act, half, t)
                    act.activation(r_row[:], ps[:, k], ACT.Square, accum_out=ssq[:, k:k + 1]
                                   ).then_inc(s["fin_sq"], 1)
                    act.wait_ge(s["fin_sq"], k + 1)
                    if half == 1:
                        act.wait_ge(s["fin_ms"], t + 1)
                        act.activation(rms[:, t:t + 1], ssq[:, t:t + 1], ACT.Sqrt, scale=1.0 / D, bias=eps_t[:]
                                       ).then_inc(s["fin_rms"], 1)


        @block.vector
        def _(dve):
            step = Steps(dve, s["dve_step"])

            def minus_hi(dst, src, hi_part):
                return dve.tensor_tensor(dst, src, hi_part.bitcast(F32), ALU.subtract)

            def scaled_minus_hi(dst, src, scale, hi_part):
                return dve.scalar_tensor_tensor(dst, src, scale, hi_part.bitcast(F32), ALU.mult, ALU.subtract)

            dve.sem_inc(s["conv_ok"], 4)
            dve.sem_inc(s["p_ok"], 6)
            dve.sem_inc(s["res_sum"], 2)
            dve.sem_inc(s["res_lo"], 2)
            dve.sem_inc(s["up_ok"], 2)
            dve.sem_inc(s["up_pad"], 4)
            for t in range(NT):
                dve.wait_ge(s["rms_ok"], t + 1)
                step.do(dve.reciprocal(rinv[:, t:t + 1], rms[:, t:t + 1]))
                dve.tensor_scalar(xn[:, t], xn[:, t], rinv[:, t:t + 1], None, ALU.mult).then_inc(s["x_scaled"], 1)
                if t == 1:
                    dve.wait_ge(raw_in[0], 32)
                    dve.tensor_copy(w_hi[:, 0], raw[:, 0]).then_inc(s["w_hi_ok"], 1)
            for c in range(KD):
                dve.wait_ge(s["h_hi_ok"], c + 1)
                scaled_minus_hi(a_lo[:, c], ps[:, c], par[:, C_MIX + c:C_MIX + c + 1], a_hi[:, c]
                                ).then_inc(s["h_lo_ok"], 1)

            with dve.Fori(0, NX // 4) as i:
                step.enter(i, 8)
                for j in range(4):
                    n = 4 * i + j
                    dve.wait_ge(s["conv_tap"], n + 1)
                    for tap in range(CONV - 2, -1, -1):
                        d = CONV - 1 - tap
                        acc = conv_acc[:, j % 2, d:]
                        ins = dve.scalar_tensor_tensor(acc, ps[:, j, 0:SEQ - d], conv_w_col(tap, n), acc,
                                                       ALU.mult, ALU.add)
                        if tap:
                            step.do(ins)
                        else:
                            ins.then_inc(s["conv_ok"], 1)
                step.leave(NX // 4)

            tile_done(dve, U_DT, 1)
            dve.tensor_copy(dtT, ps[0:HEADS, 4]).then_inc(s["dtT_ok"], 1)
            dve.wait_ge(s["dt_tr"], 1)
            dve.wait_ge(s["bcast_in"], 64)

            def tok(a):
                return a.rearrange("p (t h) -> p t h", t=NT)

            def per_head(a):
                return a.unsqueeze(1).to_broadcast([P, NT, HEADS])

            dve.tensor_tensor(tok(col("v")), tok(ps[:, 7, 0:NT * HEADS]), per_head(head_b[:, 0]), ALU.add
                              ).then_inc(s["dt_ok"], 1)
            dve.wait_ge(s["dt_exp"], 1)
            dve.tensor_scalar(col("w"), col("u"), 1.0, None, ALU.add).then_inc(s["dt_ok"], 1)
            dve.wait_ge(s["dt_ok"], 2)
            step.do(dve.tensor_scalar(col("d"), col("w"), -1.0, None, ALU.add))
            step.do(dve.tensor_scalar(col("z"), col("d"), 0.0, None, ALU.is_equal))
            step.do(dve.tensor_tensor(col("d"), col("d"), col("z"), ALU.add))
            step.did(dve.reciprocal(col("dec"), col("d")))
            step.did(dve.tensor_tensor(col("z"), col("z"), col("u"), ALU.mult))
            dve.wait_ge(s["dt_ln"], 1)
            step.do(dve.tensor_tensor(col("ln"), col("ln"), col("u"), ALU.mult))
            step.do(dve.tensor_tensor(col("ln"), col("ln"), col("dec"), ALU.mult))
            step.do(dve.tensor_tensor(col("ln"), col("ln"), col("z"), ALU.add))
            step.do(dve.scalar_tensor_tensor(col("dt"), col("v"), 0.0, col("ln"), ALU.max, ALU.add))
            dve.wait_ge(s["dt_exp"], 2)
            dve.scalar_tensor_tensor(tok(col("a")), tok(col("dt")), -1.0, per_head(head_b[:, 1]), ALU.mult, ALU.mult
                                     ).then_inc(s["dt_ok"], 1)
            dve.wait_ge(s["acs_mm"], 1)
            w = NT * HEADS
            dve.tensor_copy(col("acs"), ps[:, 7, w:2 * w]).then_inc(s["acs_ok"], 1)
            dve.wait_ge(s["acs_ok"], 1)
            dve.tensor_tensor(col("dec"), ps[:, 7, 2 * w:3 * w], col("acs"), ALU.subtract).then_inc(s["acs_ok"], 1)
            dve.tensor_copy(col("cd"), ps[:, 7, 2 * w:3 * w]).then_inc(s["acs_ok"], 1)
            dve.wait_ge(s["acs_mm"], 2)
            dve.tensor_copy(acsT, ps[0:HEADS, 6]).then_inc(s["acsT_ok"], 1)
            for c in range(1, KD, 2):
                dve.wait_ge(s["xtr_mm"], c + 1)
                dve.tensor_copy(xn[:, :, c * P:(c + 1) * P], ps[:, 4 + c % 4].rearrange("p (t n) -> p t n", t=NT)
                                ).then_inc(s["xn_odd"], 1)
            for g in range(GROUPS):
                dve.wait_ge(s["xtr_mm"], KD + g + 1)
                dve.tensor_copy(b_nat[:, :, g], ps[:, 4 + g].rearrange("p (t n) -> p t n", t=NT)
                                ).then_inc(s["xn_odd"], 1)

            def seg_sums(c):
                dve.wait_ge(seg_in[c % 2], 16 * (c // 2 + 1))
                for h in range(HEADS):
                    a = c * HEADS + h
                    dve.tensor_scalar(seg[:, c % 2, h], seg[:, c % 2, h], col("acs")[:, a:a + 1], 0.0,
                                      ALU.subtract, ALU.min).then_inc(s["seg_ok"], 1)

            def cb_masked(c):
                dve.wait_ge(s["cb_mm"], c + 1)
                if c >= 1:
                    dve.wait_ge(s["m_ok"], 2 * c)
                dve.tensor_tensor(cb_m[:], ps[:, 6, 0:GROUPS * P].rearrange("p (g l) -> p g l", g=GROUPS),
                                  tri_u[:].unsqueeze(1).to_broadcast([P, GROUPS, P]), ALU.mult).then_inc(s["cb_ok"], 1)

            def decayed_cb(c):
                dve.wait_ge(s["seg_exp"], c + 1)
                dve.wait_ge(s["cb_ok"], c + 1)
                for g in range(GROUPS):
                    m = seg[:, c % 2, g * GH:(g + 1) * GH]
                    dve.tensor_tensor(m, m, cb_m[:, g].unsqueeze(1).to_broadcast([P, GH, P]), ALU.mult
                                      ).then_inc(s["m_ok"], 1)

            def ssd_out(c):
                for g in range(GROUPS):
                    if g == 1 and c < NT - 1:
                        seg_sums(c + 1)
                    gs = slice(g * GW, (g + 1) * GW)
                    yh = yt[:, gs].rearrange("p (h d) -> p h d", h=GH)
                    xh = xsk[:, gs].rearrange("p (h d) -> p h d", h=GH)
                    ch = carry[:, gs].rearrange("p (h d) -> p h d", h=GH)
                    own = ps[:, 4:6].rearrange("p b (h x) -> p (b h) x", x=P)[:, :, 0:HD]
                    dve.wait_ge(s["diag_mm"], 2 * c + g + 1)
                    dve.wait_ge(s["xd_ok"], 3 * c + 2)
                    if c == 0:
                        dve.tensor_tensor(yh, own, xh, ALU.add).then_inc(s["y_ok"], 1)
                    else:
                        step.do(dve.tensor_tensor(yh, ps[:, 6].rearrange("p (h d) -> p h d", h=GH),
                                                  heads_of("e", c, g, HD), ALU.mult))
                        step.do(dve.tensor_tensor(yh, yh, xh, ALU.add))
                        dve.tensor_tensor(yh, own, yh, ALU.add).then_inc(s["y_ok"], 1)
                    if c < NT - 1:
                        dve.wait_ge(s["state_mm"], 2 * c + g + 1)
                        if c == 0:
                            dve.tensor_copy(carry[:, gs], ps[:, 7]).then_inc(s["carry_ok"], 1)
                        else:
                            step.do(dve.tensor_tensor(ch, ch, heads_of("cd", c, g, HD), ALU.mult))
                            dve.tensor_tensor(carry[:, gs], ps[:, 7], carry[:, gs], ALU.add).then_inc(s["carry_ok"], 1)
                    dve.wait_ge(s["y_ok"], 2 * c + g + 1)
                    dve.wait_ge(s["nat_ok"], 2 * NT)
                    dve.tensor_tensor(zy[:, c, gs], zy[:, c, gs], yt[:, gs], ALU.mult).then_inc(s["y_gated"], 1)

            dve.wait_ge(s["acs_ok"], 3)
            seg_sums(0)
            cb_masked(0)
            for c in range(NT):
                decayed_cb(c)
                if c == 0:
                    dve.wait_ge(s["decay_ok"], 3)
                ssd_out(c)
                if c < NT - 1:
                    cb_masked(c + 1)
            dve.wait_ge(s["ssd_rms"], 1)
            step.do(dve.reciprocal(rinv[:, 0:8], rms[:, 0:8]))
            for c in range(NT):
                for g in range(GROUPS):
                    y = zy[:, c, g * GW:(g + 1) * GW]
                    dve.scalar_tensor_tensor(y, y, rinv[:, 2 * c + g:2 * c + g + 1], ssdn_w[:, g * GW:(g + 1) * GW],
                                             ALU.mult, ALU.mult).then_inc(s["ssd_ok"], 1)

            def q_lo_part(p):
                dve.wait_ge(s["q_hi_ok"], 2 * p + 2)
                scaled_minus_hi(q_lo[0:HD, 0], ps[0:HD, 0], HD ** -0.5, q_hi[0:HD, 0]).then_inc(s["q_ok"], 1)
                scaled_minus_hi(q_lo[HD:P, 1], ps[HD:P, 0], HD ** -0.5, q_hi[HD:P, 1]).then_inc(s["q_ok"], 1)

            def k_lo_part(p):
                dve.wait_ge(s["k_hi_ok"], p + 1)
                minus_hi(k_lo[:], ps[:, 1], k_hi[:]).then_inc(s["k_ok"], 1)

            def softplus(p, e):
                n = 2 * p + e
                for c, j in enumerate(ORDER):
                    o, w = CHUNK[j]
                    dve.wait_ge(s["ln_ok"], 3 * n + c + 1)
                    soft = work[:, e, o:o + w]
                    step.do(dve.scalar_tensor_tensor(soft, ps[:, z_bank(e, j), 0:w], 0.0, soft, ALU.max, ALU.add))
                    step.do(dve.tensor_copy(s_hi[:, e, o:o + w], soft))
                    minus_hi(s_lo[:, e, o:o + w], soft, s_hi[:, e, o:o + w]).then_inc(s["soft_ok"], 1)

            def probs(p, e):
                n = 2 * p + e
                for c, j in enumerate(ORDER):
                    o, w = CHUNK[j]
                    dve.wait_ge(s["prob_ok"], 3 * n + c + 1 + 6)
                    if c == 0:
                        dve.wait_ge(s["av_mm"], n)
                    step.do(dve.tensor_copy(p_hi[:, o:o + w], work[:, e, o:o + w]))
                    minus_hi(p_lo[:, o:o + w], work[:, e, o:o + w], p_hi[:, o:o + w]).then_inc(s["p_ok"], 1)

            def pair(p, first=False, last=False):
                if not first:
                    probs(p - 1, 1)
                softplus(p, 0)
                softplus(p, 1)
                if not last:
                    k_lo_part(p + 1)
                if first:
                    dve.wait_ge(s["mem_rms"], 1)
                    step.do(dve.reciprocal(mem_ms[:, 2], mem_ms[:, 1]))
                    for b in range(MB):
                        dve.tensor_scalar(mem_nat[:, b], mem_nat[:, b], mem_ms[:, 2, b:b + 1], None, ALU.mult
                                          ).then_inc(s["mem_scaled"], 1)
                probs(p, 0)
                if not last:
                    q_lo_part(p + 1)

            dve.wait_ge(s["pad_ok"], 6)
            q_lo_part(0)
            k_lo_part(0)
            pair(0, first=True)
            with dve.Fori(0, 3) as i:
                step.enter(i, 2 * 2 * 9)
                for j in range(2):
                    pair(1 + j + 2 * i)
                step.leave(3)
            pair(7, last=True)
            probs(7, 1)

            def y_lo_part(c):
                dve.wait_ge(s["yh_ok"], c + 1)
                minus_hi(a_lo[:, c], ps[:, Y_BANKS[c % 3]], a_hi[:, c]).then_inc(s["yl_ok"], 1)

            for c in range(KD):
                dve.wait_ge(s["mh_ok"], 2 * (c // 2) + 2)
                scaled_minus_hi(m_lo[:, c], ps[:, MEM_BANKS[c // 2], (c % 2) * MEM:(c % 2 + 1) * MEM],
                                par[:, C_MEMKV + c:C_MEMKV + c + 1], m_hi[:, c]).then_inc(s["ml_ok"], 1)

            def sb_norm(n):
                c = SB_ORDER[n]
                dve.wait_ge(s["sb_bc"], n + 1)
                dve.scalar_tensor_tensor(ysb[:, c], ps[:, 2 + n % 2], par[:, C_SBN + c:C_SBN + c + 1], ysb[:, c],
                                         ALU.mult, ALU.mult).then_inc(s["sb_y"], 1)

            def sb_lo(n):
                c = SB_ORDER[n]
                dve.wait_ge(s["sb_hi_ok"], n + 1)
                minus_hi(b_lo[:, c], ysb[:, c], b_hi[:, c]).then_inc(s["sb_ok"], 1)

            y_lo_part(0)
            y_lo_part(1)
            dve.wait_ge(s["sb_rms"], 1)
            dve.reciprocal(r_row[:], r_row[:]).then_inc(s["sb_inv"], 1)
            dve.wait_ge(s["sb_rms"], 2)
            minus_hi(inv_hl[:, 1], r_row[:], inv_hl[:, 0]).then_inc(s["sb_inv"], 1)
            for c in range(2, KD):
                y_lo_part(c)
            for n in range(4):
                if n % 2 == 0:
                    h = n // 2
                    for b in range(MB):
                        dve.wait_ge(s["mv_hi_ok"], 2 * h + b + 1)
                        minus_hi(vm_lo[:, b, 512 * h:512 * h + 512], ps[:, 2 + 2 * h + b],
                                 vm_hi[:, b, 512 * h:512 * h + 512]).then_inc(s["mv_ok"], 1)
                sb_norm(n)
                sb_lo(n)
            for n in range(4):
                for m in range(2):
                    t = 2 * n + m
                    dve.wait_ge(s["mk_hi_ok"], t + 1)
                    minus_hi(km_lo[:, t], ps[:, m, 0:MEM], km_hi[:, t]).then_inc(s["mk_ok"], 1)
                sb_norm(4 + n)
                sb_lo(4 + n)

            def residual(u, n, n8, m, c_gain, hi_part, lo_part):
                one_tile = bass.ds(n, 1)
                tile_done(dve, u, m)
                dve.tensor_tensor(xT[:, one_tile], ps[:, m:m + 1], xT[:, one_tile], ALU.add).then_inc(s["res_sum"], 1)
                dve.wait_ge(s["res_sq"], n8 + 1)
                step.do(dve.tensor_tensor(acc_s[:], acc_s[:], sq[:, m], ALU.add))
                dve.wait_ge(s["res_hi"], n8 + 1)
                scaled_minus_hi(lo_part[:, one_tile], xT[:, one_tile], par[:, bass.ds(c_gain + n, 1)],
                                hi_part[:, one_tile]).then_inc(s["res_lo"], 1)

            def row_inverse(n):
                dve.wait_ge(s["row_rms"], n + 1)
                dve.reciprocal(r_row[:], r_row[:]).then_inc(s["row_ok"], 1)

            step.do(dve.memset(acc_s[:], 0.0))
            dve.wait_ge(s["res_ok"], 8)
            with dve.Fori(0, 4) as i:
                step.enter(i, 2)
                for m in range(2):
                    residual(U_OUT + 1 + 2 * i, 2 * i + m, 2 * i + m, m, C_MEM, h2_hi, h2_lo)
                step.leave(4)
            row_inverse(0)
            dve.wait_ge(s["row_ok"], 1)
            def sm_maxes(h):
                for q in range(2):
                    dve.wait_ge(s["sm_mm"], 2 * h + q + 1)
                    dve.tensor_reduce(smx[:, h, 0, 2 * q:2 * q + 2],
                                      ps[:, sm_bank(h, 2 * q)].rearrange("p (t m) -> p t m", t=2),
                                      AX.X, ALU.max, negate=True).then_inc(s["sm_max"], 1)

            def sm_divides(h):
                dve.wait_ge(s["sm_exp"], NT * (h + 1))
                step.do(dve.reciprocal(smx[:, h, 2], smx[:, h, 1]))
                for t in range(NT):
                    dve.tensor_scalar(sm_p[:, h, t], sm_p[:, h, t], smx[:, h, 2, t:t + 1], None, ALU.mult
                                      ).then_inc(s["sm_div"], 1)

            def pt_lo_part(h):
                for b in range(MB):
                    dve.wait_ge(s["pt_hi_ok"], 2 * h + b + 1)
                    minus_hi(pt_lo[:, h % 2, b], ps[:, pt_bank(h, b)], pt_hi[:, h % 2, b]).then_inc(s["pt_ok"], 1)

            def mo_lo_part(h):
                for m in range(2):
                    dve.wait_ge(s["mo_hi_ok"], 2 * h + m + 1)
                    minus_hi(b_lo[:, 2 * h + m], ps[:, 6 + m], b_hi[:, 2 * h + m]).then_inc(s["mo_ok"], 1)

            for h in range(MH):
                if h >= 2:
                    sm_maxes(h - 2)
                for m in range(2):
                    tile_done(dve, U_MQ + h, m)
                    if h:
                        dve.wait_ge(s["mq_ok"], 2 * (h - 1) + m + 1)
                    dve.scalar_tensor_tensor(sq[:, m], ps[:, mq_bank(h, m)], MHD ** -0.5, r_row[:], ALU.mult, ALU.mult
                                             ).then_inc(s["mq_f"], 1)
                for m in range(2):
                    c = 2 * h + m
                    dve.wait_ge(s["mq_hi_ok"], c + 1)
                    minus_hi(a_lo[:, c], sq[:, m], a_hi[:, c]).then_inc(s["mq_ok"], 1)
                if h >= 2:
                    sm_divides(h - 2)
            sm_maxes(2)
            sm_maxes(3)
            sm_divides(2)
            pt_lo_part(0)
            sm_divides(3)
            for h in range(MH):
                if h < MH - 1:
                    pt_lo_part(h + 1)
                mo_lo_part(h)
            step.do(dve.memset(acc_s[:], 0.0))
            with dve.Fori(0, 2) as i:
                step.enter(i, 4)
                for j in range(2):
                    for m in range(2):
                        n = 4 * i + 2 * j + m
                        residual(U_MO + 2 * i + j, n, KD + n, m, C_FFN, a_hi, a_lo)
                step.leave(2)
            row_inverse(1)

            step.do(dve.memset(u_pad[:, :, :, 0:FCONV - 1], 0.0))
            dve.wait_ge(s["row_ok"], 2)
            with dve.Fori(0, KF // 2) as i:
                step.enter(i, 4)
                for j in range(2):
                    n = 2 * i + j
                    for m in range(2):
                        tile_done(dve, U_UP + n, m)
                        dve.wait_ge(s["up_tap"], 2 * n + m + 1)
                        dve.tensor_tensor(u_pad[:, j, m, FCONV - 1:], ps[:, 2 * j + m], r_row[:], ALU.mult
                                          ).then_inc(s["up_pad"], 1)
                    for m in range(2):
                        dve.wait_ge(s["up_tap"], 2 * n + m + 1 + 4)
                        for tap in range(FCONV - 2, -1, -1):
                            ins = dve.scalar_tensor_tensor(u_acc[:, j, m], u_pad[:, j, m, tap:tap + SEQ],
                                                           ffn_w_col(tap, m, n), u_acc[:, j, m], ALU.mult, ALU.add)
                            if tap:
                                step.do(ins)
                            else:
                                ins.then_inc(s["up_conv"], 1)
                    dve.wait_ge(s["up_silu"], n + 1)
                    dve.wait_ge(s["up_conv"], 2 * n + 2)
                    dve.tensor_tensor(u_acc[:, j, 0], u_acc[:, j, 0], u_acc[:, j, 1], ALU.mult).then_inc(s["up_f"], 1)
                    dve.wait_ge(s["up_hi_ok"], n + 1)
                    minus_hi(ff_lo[:, bass.ds(n, 1)], u_acc[:, j, 0:1], ff_hi[:, bass.ds(n, 1)]).then_inc(s["up_ok"], 1)
                step.leave(KF // 2)

            dve.wait_ge(s["fin_in"], 16)
            for t in range(NT):
                dve.wait_ge(s["fin_sq"], NT + t + 1)
                dve.tensor_tensor(ssq[:, t:t + 1], ssq[:, t:t + 1], ssq[:, NT + t:NT + t + 1], ALU.add
                                  ).then_inc(s["fin_ms"], 1)
                dve.wait_ge(s["fin_rms"], t + 1)
                step.do(dve.reciprocal(rinv[:, t:t + 1], rms[:, t:t + 1]))
                if t == Y_BUFS:
                    dve.wait_ge(s["y_sent0"], 16)
                for half in range(2):
                    cols = slice(half * 512, (half + 1) * 512)
                    dve.scalar_tensor_tensor(y_out[:, t % Y_BUFS, cols], ps[:, NT * half + t], rinv[:, t:t + 1],
                                             fin_w[:, cols], ALU.mult, ALU.mult).then_inc(s["fin_y"], 1)

        @block.tensor
        def _(pe):
            def mm(dst, stationary, moving, start, stop, loose=False):
                return pe.matmul(dst, stationary, moving, start=start, stop=stop, skip_group_check=loose)

            def three(dst, st, mv, first, last):
                mm(dst, st[0], mv[0], first, False)
                mm(dst, st[0], mv[1], False, False)
                return mm(dst, st[1], mv[0], False, last)

            def w_tile(parity, k, m, width=P):
                o = k * 2 * P + m * P
                return w_hi[:, parity, o:o + width], w_lo[:, parity, o:o + width]

            def w_row(parity, k):
                return w_hi[:, parity, 512 * k:512 * k + 512], w_lo[:, parity, 512 * k:512 * k + 512]

            def split_in(u):
                pe.wait_ge(s["w_lo_ok"], u + 3)

            def t_unit(u, parity, banks, moving, free=None, first=True, last=True, width=SEQ, ready=None):
                split_in(u)
                for m in range(2):
                    if free is not None:
                        free(m)
                    for k in range(KD):
                        if ready is not None and m == 0:
                            ready(k)
                        ins = three(ps[:, banks[m], 0:width], w_tile(parity, k, m), moving(k),
                                    first and k == 0, last and k == KD - 1)
                    ins.then_inc(s["tile0_mm" if m == 0 else "w_used"], 1)

            def act_tiles(k):
                return a_hi[:, k], a_lo[:, k]

            def b_tiles(k):
                return b_hi[:, k], b_lo[:, k]

            def nat_unit(u, blocks, stationary, bank, k0, kn, first, last, free=None, done=None, loose=False,
                         some=None):
                parity = u % 2
                some = some or range(blocks)
                if 0 in some:
                    split_in(u)
                for t in some:
                    if free is not None:
                        free(t)
                    for k in range(kn):
                        st = stationary(k0 + k, t)
                        mv = w_row(parity, k)
                        ins = mm(ps[:, bank + t], st[0], mv[0], first and k == 0, False, loose)
                        if t == 0 and k == 0:
                            ins.then_inc(s["tile0_mm"], 1)
                        mm(ps[:, bank + t], st[0], mv[1], False, False, loose)
                        ins = mm(ps[:, bank + t], st[1], mv[0], False, last and k == kn - 1, loose)
                    if t == blocks - 1:
                        ins.then_inc(s["w_used"], 1)
                    elif done is not None:
                        ins.then_inc(done, 1)

            def flip(dst, src, n=P):
                return pe.transpose(dst, src, ident[0:n, 0:n])

            pe.sem_inc(s["w_used"], 2)
            pe.sem_inc(s["z_mm"], 6)
            pe.wait_ge(s["consts"], 10)
            def flip_x(t, c):
                ins = flip(ps[:, c, t * P:(t + 1) * P], xn[:, t, c * P:(c + 1) * P])
                if t == NT - 1:
                    ins.then_inc(s["x_tr"], 1)

            for t in range(NT):
                pe.wait_ge(s["x_scaled"], t + 1)
                if t == NT - 1:
                    pe.wait_ge(s["rows_in"], 160)
                    flip(ps[:, 7, 0:100], zy[0:100, 0, 0:P], 100)
                    flip(ps[:, 7, 100:100 + 4 * KF], zy[0:4 * KF, 1, 0:P], 4 * KF)
                    flip(ps[:, 7, 100 + 4 * KF:C_ALL], zy[0:4 * KF, 2, 0:P], 4 * KF).then_inc(s["par_tr"], 1)
                for c in range(KD - 1):
                    flip_x(t, c)
            pe.wait_ge(s["par_ok"], 1)
            for t in range(NT):
                flip_x(t, KD - 1)

            with pe.Fori(0, NX // 4) as i:
                for j in range(2):
                    t_unit(2 * i + j, j, (2 * j, 2 * j + 1), act_tiles,
                           free=lambda m: pe.wait_ge(s["conv_ok"], 4 * i + 2 * j + m + 1),
                           ready=(lambda k: pe.wait_ge(s["h_lo_ok"], k + 1)) if j == 0 else None)
            split_in(U_DT)
            for k in range(KD):
                ins = three(ps[0:HEADS, 4], w_tile(U_DT % 2, k, 0, HEADS), act_tiles(k), k == 0, k == KD - 1)
                if k == 0:
                    ins.then_inc(s["tile0_mm"], 1)
            ins.then_inc(s["w_used"], 1)

            def h_block(k, t):
                return a_hi[:, k, t * P:(t + 1) * P], a_lo[:, k, t * P:(t + 1) * P]

            def zv_unit(n, some=None):
                h, q = n // 2, n % 2

                def free(t):
                    if q == 0:
                        if h == 0:
                            pe.wait_ge(s["conv_ok"], NX + 4)
                        else:
                            pe.wait_ge(s["nat_ok"], NT * (h - 1) + t + 1)
                nat_unit(U_Z + n, NT, h_block, 0, 4 * q, 4, q == 0, q == 1, free=free,
                         done=s["nat_mm"] if q == 1 else None, some=some)

            def cb(c):
                if c >= 1:
                    pe.wait_ge(s["y_ok"], 2 * c)
                for g in range(GROUPS):
                    ins = mm(ps[:, 6, g * P:(g + 1) * P], vx[:, 8 + g, c * P:(c + 1) * P],
                             vx[:, 10 + g, c * P:(c + 1) * P], True, True)
                ins.then_inc(s["cb_mm"], 1)

            def chunk(c):
                for g in range(GROUPS):
                    gs = slice(g * GW, (g + 1) * GW)
                    if c + g:
                        pe.wait_ge(s["y_ok"], 2 * c + g)
                    if c >= 1:
                        pe.wait_ge(s["carry_ok"], 2 * (c - 1) + g + 1)
                        pe.wait_ge(s["cb_ok"], c + 1)
                        mm(ps[:, 6], vx[:, 10 + g, c * P:(c + 1) * P], carry[:, gs], True, True)
                    pe.wait_ge(s["m_ok"], 2 * c + g + 1)
                    pe.wait_ge(s["xd_ok"], 3 * c + 1)
                    for h in range(GH):
                        o = (g * GH + h) * HD
                        ins = mm(ps[:, 4 + h // 4, (h % 4) * P:(h % 4 + 1) * P], seg[:, c % 2, g * GH + h],
                                 xdt[:, c % 2, o:o + P], True, True)
                    ins.then_inc(s["diag_mm"], 1)
                    if c < NT - 1:
                        pe.wait_ge(s["xd_ok"], 3 * c + 3)
                        if c + g:
                            pe.wait_ge(s["carry_ok"], 2 * c + g)
                        mm(ps[:, 7], b_nat[:, c, g], xdd[:, gs], True, True).then_inc(s["state_mm"], 1)
                    if g == 0:
                        zv_unit(4 + c, range(0, 2))

            zv_unit(0, range(0, 1))
            pe.wait_ge(s["dtT_ok"], 1)
            for t in range(NT):
                ins = flip(ps[:, 7, t * HEADS:(t + 1) * HEADS], dtT[:, t * P:(t + 1) * P], HEADS)
            ins.then_inc(s["dt_tr"], 1)
            zv_unit(0, range(1, NT))
            pe.wait_ge(s["dt_ok"], 3)
            w = NT * HEADS
            mm(ps[:, 7, w:2 * w], tri_u[:], col("a"), True, True)
            mm(ps[:, 7, 2 * w:3 * w], ones[:], col("a"), True, True).then_inc(s["acs_mm"], 1)
            for c in range(NT):
                ins = mm(ps[0:HEADS, 6, c * P:(c + 1) * P], col("a")[:, c * HEADS:(c + 1) * HEADS], tri_u[:], True, True)
            ins.then_inc(s["acs_mm"], 1)
            zv_unit(1)
            pe.wait_ge(s["acs_ok"], 3)
            pe.wait_ge(s["acsT_ok"], 1)
            for c in range(KD):
                pe.wait_ge(s["conv_silu"], c + 3)
                if c >= 4:
                    pe.wait_ge(s["xn_even" if c % 2 == 0 else "xn_odd"], (c - 4) // 2 + 1)
                for t in range(NT):
                    ins = flip(ps[:, 4 + c % 4, t * P:(t + 1) * P], vx[:, c, t * P:(t + 1) * P])
                ins.then_inc(s["xtr_mm"], 1)
            pe.wait_ge(s["conv_silu"], NX + 2)
            for g in range(GROUPS):
                pe.wait_ge(s["xn_odd" if g else "xn_even"], 3)
                for t in range(NT):
                    ins = flip(ps[:, 4 + g, t * P:(t + 1) * P], vx[:, 8 + g, t * P:(t + 1) * P])
                ins.then_inc(s["xtr_mm"], 1)
            zv_unit(2)
            pe.wait_ge(s["xn_even"], 4)
            pe.wait_ge(s["xn_odd"], 6)
            cb(0)
            zv_unit(3)
            for c in range(NT):
                chunk(c)
                zv_unit(4 + c, range(2, NT - 1))
                if c < NT - 1:
                    cb(c + 1)
                zv_unit(4 + c, range(NT - 1, NT))

            def scores(p, e):
                n = 2 * p + e
                if e == 0:
                    pe.wait_ge(s["q_ok"], 2 * p + 2)
                    pe.wait_ge(s["k_ok"], p + 1)
                for c, j in enumerate(ORDER):
                    bank = z_bank(e, j)
                    pe.wait_ge(s["prob_ok"], 3 * n + c + 1)
                    for b in BLOCKS[j]:
                        o = (b == 3) * WID[2]
                        dst = ps[:, bank, o:o + WID[b]]
                        key = slice(b * P, (b + 1) * P)
                        mm(dst, k_hi[:, key], q_hi[:, e, START[b]:], b != 3, False, True)
                        mm(dst, k_hi[:, key], q_lo[:, e, START[b]:], False, False, True)
                        mm(dst, k_lo[:, key], q_hi[:, e, START[b]:], False, False, True)
                        if b == 3:
                            ins = mm(ps[:, bank, o:o + 2 * P], ident_b[:], neg_b[:], False, False, True)
                        else:
                            ins = mm(ps[:, bank, o:o + P], ident_b[:], neg_b[:, P:2 * P], False, False, True)
                    ins.then_inc(s["z_mm"], 1)

            def stick_sums(p, e):
                n = 2 * p + e
                for c, j in enumerate(ORDER):
                    bank = z_bank(e, j)
                    pe.wait_ge(s["soft_ok"], 3 * n + c + 1)
                    for b in BLOCKS[j]:
                        for src in range(b, 4):
                            o = (b == 3) * WID[2] + START[src] - START[b]
                            for part in (s_hi, s_lo):
                                ins = mm(ps[:, bank, o:o + WID[src]], (neg_tri if src == b else neg_one)[:],
                                         part[:, e, OFF[src]:OFF[src] + WID[src]], False, False, True)
                    ins.then_inc(s["cs_mm"], 1)

            def attend(p, e):
                n = 2 * p + e
                if e == 0:
                    pe.wait_ge(s["o_ok"], p)
                    pe.wait_ge(s["v_ok"], p + 1)
                side = slice(e * HD, e * HD + P)
                vh = v_hi[:].rearrange("p t a d -> p t (a d)")
                vl = v_lo[:].rearrange("p t a d -> p t (a d)")
                for c, j in enumerate(ORDER):
                    pe.wait_ge(s["p_ok"], 3 * n + c + 1 + 6)
                    for b in BLOCKS[j]:
                        dst = ps[:, 1, START[b]:]
                        src = slice(OFF[b], OFF[b] + WID[b])
                        mm(dst, vh[:, b, side], p_hi[:, src], e == 0 and c == 0 and b == 2, False, True)
                        mm(dst, vh[:, b, side], p_lo[:, src], False, False, True)
                        ins = mm(dst, vl[:, b, side], p_hi[:, src], False, False, True)
                ins.then_inc(s["av_mm"], 1)

            def flip_memory():
                pe.wait_ge(s["mem_scaled"], MB)
                pe.wait_ge(s["q_ok"], 2 * PAIRS)
                for b in range(4):
                    if b == 1:
                        pe.wait_ge(s["prob_ok"], 3 * (HEADS - 1) + 6)
                    for c in range(2):
                        for t in range(MB):
                            o = c * MEM + t * P
                            ins = flip(ps[:, MEM_BANKS[b], o:o + P],
                                       mem_nat[:, t, (2 * b + c) * P:(2 * b + c + 1) * P])
                    ins.then_inc(s["mtr_mm"], 1)

            def pair(p, u0=None, i=0, first=False):
                scores(p, 0)
                scores(p, 1)
                if not first:
                    attend(p - 1, 1)
                if u0 is not None:
                    t_unit(u0 + 2 * i, u0 % 2, (0, 1), act_tiles,
                           free=(lambda m: pe.wait_ge(s["o_ok"], p) if m else None) if not first else None)
                stick_sums(p, 0)
                stick_sums(p, 1)
                if u0 is not None:
                    pe.wait_ge(s["k_ok"], p + 2)
                else:
                    flip_memory()
                attend(p, 0)

            pe.wait_ge(s["nat_ok"], 4 * NT)
            t_unit(U_QK, U_QK % 2, (0, 1), act_tiles)
            pe.wait_ge(s["y_ok"], 2 * NT)
            pe.wait_ge(s["consts_r"], 4)
            pair(0, U_QK + 1, first=True)
            with pe.Fori(0, 3) as i:
                for j in range(2):
                    pair(1 + j + 2 * i, U_QK + 2 + j, i)
            pair(7)

            attend(7, 1)
            pe.wait_ge(s["prob_ok"], 3 * HEADS + 6)

            def flip_y(c):
                if c == 0:
                    pe.wait_ge(s["ssd_ok"], 8)
                elif c == 1:
                    pe.wait_ge(s["o_ok"], PAIRS)
                elif c >= 3:
                    pe.wait_ge(s["yl_ok"], c - 2)
                for t in range(NT):
                    ins = flip(ps[:, Y_BANKS[c % 3], t * P:(t + 1) * P], zy[:, t, c * P:(c + 1) * P])
                ins.then_inc(s["ytr_mm"], 1)

            def head_sums(n):
                c = SB_ORDER[n]
                pe.wait_ge(s["sb_sq"], n + 1)
                mm(ps[:, 6], head_sel[:, HEADS - 2 - 2 * c:HEADS - 2 - 2 * c + P], sq[:, n % 2], n == 0, n == KD - 1
                   ).then_inc(s["sb_mm"], 1)

            def head_inverses(n):
                c = SB_ORDER[n]
                if n == 0:
                    pe.wait_ge(s["sb_inv"], 2)
                    pe.wait_ge(s["head_rows_ok"], 1)
                    pe.wait_ge(s["mv_ok"], MB)
                if n >= 2:
                    pe.wait_ge(s["sb_y"], n - 1)
                sel = head_rows[:, c * P:(c + 1) * P]
                mm(ps[:, 2 + n % 2], sel, inv_hl[:, 0], True, False)
                mm(ps[:, 2 + n % 2], sel, inv_hl[:, 1], False, True).then_inc(s["sb_bc"], 1)

            def m_block(k, t):
                return m_hi[:, k, t * P:(t + 1) * P], m_lo[:, k, t * P:(t + 1) * P]

            def m_tiles(k):
                return m_hi[:, k], m_lo[:, k]

            for n in range(4):
                h, q = n // 2, n % 2
                if n == 0:
                    pe.wait_ge(s["ml_ok"], KD)
                nat_unit(U_MV + n, MB, m_block, 2 + 2 * h, 4 * q, 4, q == 0, q == 1,
                         done=s["mv_mm"] if q == 1 else None)
                if n == 0:
                    flip_y(0)
                    flip_y(1)
                    for c in range(KD):
                        head_sums(c)
                    flip_y(2)
                    flip_y(3)
                if n == 1:
                    for c in range(4, KD):
                        flip_y(c)
                if n == 2:
                    head_inverses(0)
                    head_inverses(1)
            head_inverses(2)
            head_inverses(3)
            for n in range(4):
                u = U_MK + n
                t_unit(u, u % 2, (0, 1), m_tiles, width=MEM,
                       free=(lambda m: pe.wait_ge(s["mk_ok"], 2 * (n - 1) + m + 1)) if n else None)
                head_inverses(4 + n)
                pe.wait_ge(xblk_in[n % 2], 16 * (n // 2 + 1))
                for q in range(2):
                    if n:
                        pe.wait_ge(s["res_ok"], 2 * n + q - 1)
                    for c in range(4):
                        ins = flip(ps[:, 6 + q, c * P:(c + 1) * P], x_blk[:, n % 2, (4 * q + c) * P:(4 * q + c + 1) * P])
                    ins.then_inc(s["res_tr"], 1)

            def row_sums(n):
                pe.wait_ge(s["res_lo"], KD * (n + 1) + 2)
                mm(ps[:, 6], ones[:], acc_s[:], True, True).then_inc(s["row_mm"], 1)

            pe.wait_ge(s["mk_ok"], 8)
            pe.wait_ge(s["yl_ok"], KD)
            with pe.Fori(0, 4) as i:
                t_unit(U_OUT + 2 * i, U_OUT % 2, (0, 1), act_tiles, last=False,
                       free=lambda m: pe.wait_ge(s["res_sum"], 2 * i + m + 1))
                pe.wait_ge(s["sb_ok"], KD)
                t_unit(U_OUT + 1 + 2 * i, (U_OUT + 1) % 2, (0, 1), b_tiles, first=False)

            def h2_tiles(k):
                return h2_hi[:, k], h2_lo[:, k]

            def memory_q(h):
                u = U_MQ + h
                t_unit(u, u % 2, (mq_bank(h, 0), mq_bank(h, 1)), h2_tiles,
                       free=[lambda m: pe.wait_ge(s["res_sum"], KD + m + 1), None,
                             lambda m: pe.wait_ge(s["mq_f"], m + 1),
                             lambda m: pe.wait_ge(s["mq_f"], 4 + m + 1)][h],
                       ready=None if h else (lambda k: pe.wait_ge(s["res_lo"], k + 1 + 2)))

            def memory_scores(h):
                pe.wait_ge(s["mq_ok"], 2 * h + 2)
                if h == 3:
                    pe.wait_ge(s["mq_f"], 8)
                for t in range(NT):
                    for k in range(2):
                        c = 2 * h + k
                        o = (t % 2) * MEM
                        ins = three(ps[:, sm_bank(h, t), o:o + MEM], h_block(c, t), (km_hi[:, c], km_lo[:, c]),
                                    k == 0, k == 1)
                    if t % 2:
                        ins.then_inc(s["sm_mm"], 1)

            memory_q(0)
            row_sums(0)
            memory_q(1)
            for h in range(2, MH):
                memory_scores(h - 2)
                memory_q(h)
            memory_scores(2)
            memory_scores(3)
            def flip_softmax(h):
                pe.wait_ge(s["sm_div"], NT * (h + 1))
                if h >= 2:
                    pe.wait_ge(s["pt_ok"], 2 * (h - 1))
                for b in range(MB):
                    for t in range(NT):
                        ins = flip(ps[:, pt_bank(h, b), t * P:(t + 1) * P], sm_p[:, h, t, b * P:(b + 1) * P])
                    ins.then_inc(s["pt_mm"], 1)

            flip_softmax(0)
            for h in range(MH):
                if h < MH - 1:
                    flip_softmax(h + 1)
                if h == 0:
                    pe.wait_ge(s["sm_exp"], 3 * NT)
                for m in range(2):
                    if h:
                        pe.wait_ge(s["mo_ok"], 2 * (h - 1) + m + 1)
                    for b in range(MB):
                        pe.wait_ge(s["pt_ok"], 2 * h + b + 1)
                        o = h * MHD + m * P
                        ins = three(ps[:, 6 + m], (vm_hi[:, b, o:o + P], vm_lo[:, b, o:o + P]),
                                    (pt_hi[:, h % 2, b], pt_lo[:, h % 2, b]), b == 0, b == 1)
                    ins.then_inc(s["o_mm"], 1)
            pe.wait_ge(s["sm_exp"], 4 * NT)
            with pe.Fori(0, 2) as i:
                for j in range(2):
                    u0 = U_MO + j
                    t_unit(u0 + 2 * i, u0 % 2, (0, 1), b_tiles,
                           free=lambda m: pe.wait_ge(s["res_sum"], KD + 4 * i + 2 * j + m + 1),
                           ready=None if j else (lambda k: pe.wait_ge(s["mo_ok"], k + 1)))
            def up_unit(j, i, ready=None):
                u0 = U_UP + j
                t_unit(u0 + 2 * i, u0 % 2, (2 * j, 2 * j + 1), act_tiles, ready=ready,
                       free=lambda m: pe.wait_ge(s["up_pad"], 4 * i + 2 * j + m + 1))

            pe.wait_ge(s["res_sum"], 2 * KD + 2)
            up_unit(0, 0, lambda k: pe.wait_ge(s["res_lo"], KD + k + 1 + 2))
            row_sums(1)
            up_unit(1, 0)
            with pe.Fori(1, KF // 2) as i:
                for j in range(2):
                    up_unit(j, i)
            pe.wait_ge(s["up_pad"], 2 * KF + 4)
            for half in range(2):
                for t in range(NT):
                    for c in range(4):
                        mm(ps[:, NT * half + t, c * P:(c + 1) * P], xT[:, 4 * half + c, t * P:(t + 1) * P],
                           ident[:], c == 0, False, True)
            pe.wait_ge(s["up_ok"], KF + 2)

            def ff_block(k, t):
                return ff_hi[:, k, t * P:(t + 1) * P], ff_lo[:, k, t * P:(t + 1) * P]

            def down_unit(half, n):
                end = n == len(DOWN_K) - 1
                nat_unit(U_DOWN + half * len(DOWN_K) + n, NT, ff_block, NT * half, DOWN_AT[n], DOWN_K[n], False, end,
                         done=s["down_mm"] if end else None, loose=True)

            for half in range(2):
                for n in range(len(DOWN_K)):
                    down_unit(half, n)


_NAMES = ["x", "mem", "norm_mix_w", "w_in", "conv_ssd_w", "conv_ssd_b", "dt_bias", "a_log", "d_skip",
          "ssd_norm_w", "sb_norm_w", "w_out", "norm_mem_w", "norm_memkv_w", "w_mq", "w_mk", "w_mv", "w_mo",
          "norm_ffn_w", "w_up", "conv_ffn_w", "conv_ffn_b", "w_down", "norm_final_w"]


def kernel(**inputs):
    import numpy as np
    import concourse.bacc as bacc
    from concourse.bass_utils import run_bass_kernel_spmd

    nc = bacc.Bacc("TRN2", target_bir_lowering=False, num_devices=1)
    arrays, args = {}, []
    for name in _NAMES:
        a = np.ascontiguousarray(inputs[name])
        arrays["in_" + name] = a
        args.append(nc.dram_tensor("in_" + name, a.shape, mybir.dt.from_np(a.dtype), kind="ExternalInput").ap())
    args.append(nc.dram_tensor("acs_dram", (NT, HEADS, P), F32, kind="Internal").ap())
    args.append(nc.dram_tensor("out", (1, SEQ, D), F32, kind="ExternalOutput").ap())
    hymba_layer(nc, *args)
    r = run_bass_kernel_spmd(nc, [arrays], core_ids=[0])
    return r.results[0]["out"]
```
